# Optimizing a Trainium2 kernel written in Bass

```python
import math
import jax, jax.numpy as jnp
from jax import lax
import numpy as np

D_MODEL = 1024
BATCH = 1
SEQ = 512
DEPTH = 2

N_MIXERS = 2
D_FF = 2816
NORM_EPS = 1e-6
CHUNK = 64

HG_DK = 128
HG_HEADS = D_MODEL // HG_DK
HG_DV = D_MODEL // HG_HEADS
HG_IN = 4 * D_MODEL
N_HG_LAYERS = (DEPTH + 1) // 2

GD_QK_HEADS = 8
GD_V_HEADS = 16
GD_DK = 128
GD_DV = 128
GD_KEY = GD_QK_HEADS * GD_DK
GD_VAL = GD_V_HEADS * GD_DV
GD_QKV = 2 * GD_KEY + GD_VAL
GD_CONV = 4
GD_IN = GD_QKV + GD_VAL + 2 * GD_V_HEADS
N_GD_LAYERS = DEPTH // 2

kernel_name = "hgrn2_gdn_macaron_sandwich_trunk"

def _rmsnorm(x, gain):
    xf = x.astype(jnp.float32)
    y = xf * lax.rsqrt(jnp.mean(xf * xf, axis=-1, keepdims=True) + NORM_EPS)
    return (y * gain.astype(jnp.float32)).astype(x.dtype)

def _gated_rmsnorm(o, gate, gain):
    y = o * lax.rsqrt(jnp.mean(o * o, axis=-1, keepdims=True) + NORM_EPS)
    return y * gain.astype(jnp.float32) * jax.nn.silu(gate)

def _l2norm(x):
    return x * lax.rsqrt(jnp.sum(x * x, axis=-1, keepdims=True) + NORM_EPS)

def _swiglu(x, w_in, w_out):
    gate, up = jnp.split(x @ w_in, 2, axis=-1)
    return (jax.nn.silu(gate) * up) @ w_out

def _to_chunks(x):
    B, T, H, d = x.shape
    return x.reshape(B, T // CHUNK, CHUNK, H, d).transpose(0, 3, 1, 2, 4)

def _to_chunks_scalar(x):
    B, T, H = x.shape
    return x.reshape(B, T // CHUNK, CHUNK, H).transpose(0, 3, 1, 2)

def _from_chunks(x):
    B, H, N, C, d = x.shape
    return x.transpose(0, 2, 3, 1, 4).reshape(B, N * C, H, d)

def _causal_conv(x, w):
    K, C = w.shape
    return lax.conv_general_dilated(
        x, w[:, None, :], window_strides=(1,), padding=[(K - 1, 0)],
        dimension_numbers=("NWC", "WIO", "NWC"), feature_group_count=C)

def _hgrn2(h, w_in, lower_bound, norm_gain, w_out):
    B, T, _ = h.shape
    q, f, i, g = jnp.split((h @ w_in).astype(jnp.float32), 4, axis=-1)
    q = jax.nn.silu(q)
    forget = lower_bound + (1.0 - lower_bound) * jax.nn.sigmoid(f)
    k = 1.0 - forget
    log_f = jnp.log(forget)
    q_c, k_c, v_c, lf_c = [_to_chunks(t.reshape(B, T, HG_HEADS, -1)) for t in (q, k, i, log_f)]
    b = jnp.cumsum(lf_c, axis=-2)
    b_mid = b[..., CHUNK // 2:CHUNK // 2 + 1, :]
    causal = jnp.tril(jnp.ones((CHUNK, CHUNK), dtype=bool))
    scores = jnp.einsum("bhnck,bhnsk->bhncs", q_c * jnp.exp(b - b_mid), k_c * jnp.exp(b_mid - b))
    o_intra = jnp.einsum("bhncs,bhnsv->bhncv", jnp.where(causal, scores, 0.0), v_c)
    b_last = b[..., -1:, :]
    q_inter = q_c * jnp.exp(b)
    k_state = k_c * jnp.exp(b_last - b)
    decay = jnp.exp(b_last[..., 0, :])

    def step(S, xs):
        qn, kn, vn, dn = xs
        o = jnp.einsum("bhck,bhkv->bhcv", qn, S)
        S = dn[..., :, None] * S + jnp.einsum("bhsk,bhsv->bhkv", kn, vn)
        return S, o

    S0 = jnp.zeros((B, HG_HEADS, HG_DK, HG_DV), jnp.float32)
    xs = tuple(jnp.moveaxis(t, 2, 0) for t in (q_inter, k_state, v_c, decay))
    _, o_inter = lax.scan(step, S0, xs)
    o = _from_chunks(o_intra + jnp.moveaxis(o_inter, 0, 2))
    o = _gated_rmsnorm(o, g.reshape(B, T, HG_HEADS, HG_DV), norm_gain)
    return o.reshape(B, T, HG_HEADS * HG_DV).astype(h.dtype) @ w_out

def _gated_deltanet(h, w_in, conv_w, a_log, dt_bias, norm_gain, w_out):
    B, T, _ = h.shape
    proj = (h @ w_in).astype(jnp.float32)
    qkv = jax.nn.silu(_causal_conv(proj[..., :GD_QKV], conv_w.astype(jnp.float32)))
    z = proj[..., GD_QKV:GD_QKV + GD_VAL]
    beta = jax.nn.sigmoid(proj[..., GD_QKV + GD_VAL:GD_QKV + GD_VAL + GD_V_HEADS])
    a = proj[..., GD_QKV + GD_VAL + GD_V_HEADS:]
    g = -jnp.exp(a_log.astype(jnp.float32)) * jax.nn.softplus(a + dt_bias)
    rep = GD_V_HEADS // GD_QK_HEADS
    q = _l2norm(qkv[..., :GD_KEY].reshape(B, T, GD_QK_HEADS, GD_DK)) * (GD_DK ** -0.5)
    k = _l2norm(qkv[..., GD_KEY:2 * GD_KEY].reshape(B, T, GD_QK_HEADS, GD_DK))
    v = qkv[..., 2 * GD_KEY:].reshape(B, T, GD_V_HEADS, GD_DV)
    q_c = _to_chunks(jnp.repeat(q, rep, axis=2))
    k_c = _to_chunks(jnp.repeat(k, rep, axis=2))
    v_c = _to_chunks(v)
    beta_c = _to_chunks_scalar(beta)
    G = jnp.cumsum(_to_chunks_scalar(g), axis=-1)
    incl = jnp.tril(jnp.ones((CHUNK, CHUNK), dtype=bool))
    strict = jnp.tril(jnp.ones((CHUNK, CHUNK), dtype=bool), k=-1)
    gamma = jnp.exp(jnp.where(incl, G[..., :, None] - G[..., None, :], -jnp.inf))
    kk = jnp.einsum("bhnck,bhnsk->bhncs", k_c, k_c)
    a_mat = jnp.where(strict, kk * gamma * beta_c[..., :, None], 0.0)
    eye = jnp.eye(CHUNK, dtype=jnp.float32)
    t_mat = lax.linalg.triangular_solve(a_mat + eye, jnp.broadcast_to(eye, a_mat.shape),
                                        left_side=True, lower=True, unit_diagonal=True)
    u = jnp.einsum("bhncs,bhnsv->bhncv", t_mat, v_c * beta_c[..., None])
    w = jnp.einsum("bhncs,bhnsk->bhnck", t_mat, k_c * (beta_c * jnp.exp(G))[..., None])
    qk = jnp.einsum("bhnck,bhnsk->bhncs", q_c, k_c) * gamma
    q_g = q_c * jnp.exp(G)[..., None]
    k_g = k_c * jnp.exp(G[..., -1:] - G)[..., None]
    decay = jnp.exp(G[..., -1])

    def step(S, xs):
        un, wn, qkn, qn, kn, dn = xs
        v_new = un - jnp.einsum("bhck,bhkv->bhcv", wn, S)
        o = jnp.einsum("bhck,bhkv->bhcv", qn, S) + jnp.einsum("bhcs,bhsv->bhcv", qkn, v_new)
        S = dn[..., None, None] * S + jnp.einsum("bhsk,bhsv->bhkv", kn, v_new)
        return S, o

    S0 = jnp.zeros((B, GD_V_HEADS, GD_DK, GD_DV), jnp.float32)
    xs = tuple(jnp.moveaxis(t, 2, 0) for t in (u, w, qk, q_g, k_g, decay))
    _, o = lax.scan(step, S0, xs)
    o = _from_chunks(jnp.moveaxis(o, 0, 2))
    o = _gated_rmsnorm(o, z.reshape(B, T, GD_V_HEADS, GD_DV), norm_gain)
    return o.reshape(B, T, GD_VAL).astype(h.dtype) @ w_out

def setup_inputs(seed: int = 0) -> dict:
    key = jax.random.key(seed)
    ks = jax.random.split(key, 16)

    def nrm(k, shape, scale):
        return jax.random.normal(k, shape, jnp.float32) * scale

    dt = jnp.exp(jax.random.uniform(ks[13], (N_GD_LAYERS, GD_V_HEADS), jnp.float32,
                                    minval=math.log(1e-3), maxval=math.log(1e-1)))
    return {
        "x": nrm(ks[0], (BATCH, SEQ, D_MODEL), 1.0),
        "norm_gains": 1.0 + nrm(ks[1], (DEPTH, 6, D_MODEL), 0.02),
        "ffn1_w_in": nrm(ks[2], (DEPTH, D_MODEL, 2 * D_FF), D_MODEL ** -0.5),
        "ffn1_w_out": nrm(ks[3], (DEPTH, D_FF, D_MODEL), D_FF ** -0.5),
        "ffn2_w_in": nrm(ks[4], (DEPTH, D_MODEL, 2 * D_FF), D_MODEL ** -0.5),
        "ffn2_w_out": nrm(ks[5], (DEPTH, D_FF, D_MODEL), D_FF ** -0.5),
        "hg_w_in": nrm(ks[6], (N_HG_LAYERS, D_MODEL, HG_IN), D_MODEL ** -0.5),
        "hg_lower_bounds": 1.0 + nrm(ks[7], (N_HG_LAYERS, HG_HEADS * HG_DK), 0.1),
        "hg_norm_gain": 1.0 + nrm(ks[8], (N_HG_LAYERS, HG_DV), 0.02),
        "hg_w_out": nrm(ks[9], (N_HG_LAYERS, HG_HEADS * HG_DV, D_MODEL), D_MODEL ** -0.5),
        "gd_w_in": nrm(ks[10], (N_GD_LAYERS, D_MODEL, GD_IN), D_MODEL ** -0.5),
        "gd_conv_w": nrm(ks[11], (N_GD_LAYERS, GD_CONV, GD_QKV), GD_CONV ** -0.5),
        "gd_a_log": jnp.log(jax.random.uniform(ks[12], (N_GD_LAYERS, GD_V_HEADS), jnp.float32,
                                                minval=1.0, maxval=16.0)),
        "gd_dt_bias": dt + jnp.log(-jnp.expm1(-dt)),
        "gd_norm_gain": 1.0 + nrm(ks[14], (N_GD_LAYERS, GD_DV), 0.02),
        "gd_w_out": nrm(ks[15], (N_GD_LAYERS, GD_VAL, D_MODEL), GD_VAL ** -0.5),
    }

def reference(x, norm_gains, ffn1_w_in, ffn1_w_out, ffn2_w_in, ffn2_w_out,
              hg_w_in, hg_lower_bounds, hg_norm_gain, hg_w_out,
              gd_w_in, gd_conv_w, gd_a_log, gd_dt_bias, gd_norm_gain, gd_w_out):
    lb = jnp.cumsum(jax.nn.softmax(hg_lower_bounds.astype(jnp.float32), axis=0), axis=0)
    lb = lb - lb[0]
    for i in range(DEPTH):
        ng = norm_gains[i]
        x = x + 0.5 * _rmsnorm(_swiglu(_rmsnorm(x, ng[0]), ffn1_w_in[i], ffn1_w_out[i]), ng[1])
        h = _rmsnorm(x, ng[2])
        j = i // N_MIXERS
        if i % N_MIXERS == 0:
            m = _hgrn2(h, hg_w_in[j], lb[j], hg_norm_gain[j], hg_w_out[j])
        else:
            m = _gated_deltanet(h, gd_w_in[j], gd_conv_w[j], gd_a_log[j], gd_dt_bias[j],
                                gd_norm_gain[j], gd_w_out[j])
        x = x + _rmsnorm(m, ng[3])
        x = x + 0.5 * _rmsnorm(_swiglu(_rmsnorm(x, ng[4]), ffn2_w_in[i], ffn2_w_out[i]), ng[5])
    return x


_drawn_inputs = setup_inputs


def setup_inputs(seed=0):
    import zlib

    import numpy as np

    out = dict(_drawn_inputs(seed))
    spreads = {}
    factors = {}
    for name, (base, spread) in spreads.items():
        noise = np.random.default_rng([zlib.crc32(name.encode()), seed]).standard_normal(out[name].shape)
        drawn = base * np.exp(spread * noise) if base else spread * noise
        out[name] = __import__('jax').numpy.asarray(drawn.astype(out[name].dtype))
    for name, factor in factors.items():
        out[name] = (out[name] * factor).astype(out[name].dtype)
    return out
```

```python
import concourse.bass as bass
from concourse import mybir
from contextlib import ExitStack

P = 128
TOK = 512
D = 1024
KD = D // P
FF = 2816
KF = FF // P
UNIT = KD * P
RING = 4
HEADS = 8
CH = 64
NCH = TOK // CH
NT = TOK // P
GROUPS = 8
VH = 16
TAPS = 4
LEVELS = 7
AB = 48
CUTS = {"ffn": [0, 6, 12, 17, 22], "hg": [0, 8], "gd": [0, 8, 16]}


def trunk(nc, A, out, kinds=("ffn", "hg", "ffn", "ffn", "gd", "ffn")):
    f32 = mybir.dt.float32
    f32r = mybir.dt.float32r
    u8 = mybir.dt.int8
    ALU = mybir.AluOpType
    ACT = mybir.ActivationFunctionType
    AX = mybir.AxisListType
    IN_UNITS = {"ffn": 2 * KF, "hg": 4 * HEADS, "gd": 1 + 6 * GROUPS}
    N_UNITS = {k: n + KD * (len(CUTS[k]) - 1) for k, n in IN_UNITS.items()}
    first_unit, total = [], 0
    for kind in kinds:
        first_unit.append(total)
        total += N_UNITS[kind]
    ffn_no = {s: n for n, s in enumerate(s for s, k in enumerate(kinds) if k == "ffn")}
    LAST = len(kinds)

    ctx = ExitStack()
    with ctx:
        def sb(name, shape, dt=f32):
            return ctx.enter_context(nc.sbuf_tensor(name, shape, dt))

        def sem(name):
            return ctx.enter_context(nc.semaphore(name))

        x = sb("resid", [P, KD, TOK])
        h_hi = sb("h_hi", [P, KD, TOK], f32r)
        with nc.sbuf_tensor("m", [P, KD, TOK], f32) as m:
            pass
        h_lo = sb("h_lo", [P, KD, TOK], f32r)
        raw = sb("raw", [P, RING, UNIT])
        w_hi = sb("w_hi", [P, RING, UNIT], f32r)
        w_lo = sb("w_lo", [P, RING, UNIT], f32r)
        gains = sb("gain_table", [P, 12 * KD])
        half_gains = sb("half_gains", [P, 12 * KD])
        ones = sb("ones", [P, P])
        eps = sb("eps", [P, 1])
        sq = sb("sq", [P, 2, TOK])
        acc = sb("acc", [P, TOK])
        rms = sb("rms", [P, 2, TOK])
        y = sb("y", [P, 2, TOK])
        gate = sb("gate", [P, TOK])
        up = sb("up", [P, TOK])
        ident = sb("ident", [P, P])
        upper = sb("upper", [P, P])
        with ExitStack() as region:
            def part(name, shape, dt=f32):
                return region.enter_context(nc.sbuf_tensor(name, shape, dt))
            act_hi = part("act_hi", [P, KF, TOK], f32r)
            act_lo = part("act_lo", [P, KF, TOK], f32r)
        with ExitStack() as region:
            def part(name, shape, dt=f32):
                return region.enter_context(nc.sbuf_tensor(name, shape, dt))
            o_hi = part("o_hi", [P, HEADS, TOK], f32r)
            o_lo = part("o_lo", [P, HEADS, TOK], f32r)
            f_in, g_in = gate, up
            (sig, forget, key, logf, b, b_mid, b_end, e_pos, e_neg, e_all, e_end, v_fm, q_in, q_act, g_act,
             q_cen, k_cen, q_int, k_end, osq, o_rms, o_fm) = [part(n, [P, TOK]) for n in (
                "sig", "forget", "key", "logf", "b", "b_mid", "b_end", "e_pos", "e_neg", "e_all", "e_end", "v_fm",
                "q_in", "q_act", "g_act", "q_cen", "k_cen", "q_int", "k_end", "osq", "o_rms", "o_fm")]
            v_tok = part("v_tok", [P, NT, P])
            k_tok = part("k_tok", [P, NT, P])
            probs = part("probs", [P, NT, P])
            state = part("state", [P, NCH - 1, P])
            scan_keep = part("scan_keep", [P, TOK])
            causal = part("causal", [P, P])
            bound = part("bound", [P, HEADS])
            bound_rest = part("bound_rest", [P, HEADS])
            bound_tmp = part("bound_tmp", [P, 3, HEADS])
            hg_gain = part("hg_gain", [P, 1])
        with ExitStack() as region:
            def part(name, shape, dt=f32):
                return region.enter_context(nc.sbuf_tensor(name, shape, dt))
            gd_o = part("gd_o", [P, VH, TOK])
            with ExitStack() as inner:
                def late(name, shape, dt=f32):
                    return inner.enter_context(nc.sbuf_tensor(name, shape, dt))
                go_lo_a = late("go_lo_a", [P, KD, TOK], f32r)
                go_hi_b = late("go_hi_b", [P, KD, TOK], f32r)
                go_lo_b = late("go_lo_b", [P, KD, TOK], f32r)
            pre = part("pre", [P, TAPS - 1 + TOK])
            q_a = part("q_a", [P, TOK])
            k_a = part("k_a", [P, TOK])
            v_a = part("v_a", [P, 2, TOK])
            z_a = part("z_a", [P, 2, TOK])
            vt = part("vt", [P, 2, NT, P])
            g_bc = part("g_bc", [P, 2, TOK])
            q_g = part("q_g", [P, 2, TOK])
            attn = part("attn", [P, 2, NT, P])
            neg_at = part("neg_at", [P, 2, NT, P])
            inv = part("inv", [P, 2, NT, P])
            inv_t = part("inv_t", [P, 2, NT, P])
            prod_at = part("prod_at", [P, 2, NT, P])
            resid_v = part("resid_v", [P, 2, P])
            v_new = part("v_new", [P, 2, P])
            v_dec = part("v_dec", [P, 2, P])
            mem = part("mem", [P, 2, 2, P])
            low_mask = part("low_mask", [P, LEVELS, P], u8)
            up_mask = part("up_mask", [P, LEVELS, P], u8)
            pair_mask = part("pair_mask", [P, P])
            tab = part("tab", [P, 6, NT, VH])
            spare = part("spare", [P, 1])
            gtab = part("gtab", [P, 6, NT, 2])
            conv_w = part("conv_w", [P, GROUPS, 4, TAPS])
            gd_gain = part("gd_gain", [P, 1])
            gd_ab = part("gd_ab", [AB, 2])
            ea = part("ea", [AB, 1])
        qn, kn = sq[:, 0, :], sq[:, 1, :]
        ab_in = attn[:].rearrange("p e t c -> p (e t c)")[0:AB, 0:TOK]
        ab_exp = attn[:].rearrange("p e t c -> p (e t c)")[0:AB, TOK:2 * TOK]
        keep_rows = neg_at[:].rearrange("p e t c -> p (e t c)")[0:AB, 0:TOK]
        g_step = neg_at[:].rearrange("p e t c -> p (e t c)")[0:AB, TOK:2 * TOK]
        g_row_tile = inv[:].rearrange("p e t c -> p (e t c)")[0:AB, 0:TOK]
        tab_t = inv[:].rearrange("p e t c -> p (e t c)")[:, TOK:TOK + NT * AB].rearrange("p (t h) -> p t h", h=AB)
        kt = acc
        silu = y[:, 0, :]
        prod = y[:, 1, :]
        bank = [ctx.enter_context(nc.psum_tensor(f"bank{i}", [P, TOK], f32)) for i in range(8)]

        raw_loaded = [sem(f"raw_loaded{i}") for i in range(RING)]
        hi_split = sem("hi_split")
        lo_split = sem("lo_split")
        unit_used = sem("unit_used")
        x_loaded = sem("x_loaded")
        const_loaded = sem("const_loaded")
        const_made = sem("const_made")
        sq_done = sem("sq_done")
        acc_done = sem("acc_done")
        sum_ready = sem("sum_ready")
        rms_logged = sem("rms_logged")
        rms_ready = sem("rms_ready")
        m_copied = sem("m_copied")
        y_scaled = sem("y_scaled")
        x_ready = sem("x_ready")
        h_hi_ready = sem("h_hi_ready")
        h_ready = sem("h_ready")
        gate_scaled = sem("gate_scaled")
        up_scaled = sem("up_scaled")
        gate_silu = sem("gate_silu")
        act_mul = sem("act_mul")
        act_hi_ready = sem("act_hi_ready")
        act_ready = sem("act_ready")
        stored = sem("stored")
        ab_loaded = sem("ab_loaded")
        hg_loaded = sem("hg_loaded")
        x_gate = sem("x_gate")
        (qk_summed, v_trans, k_trans, kk_made, qk_made, x_trans, p_made, tt_made, xx_made, ks_made, wr_made, og_made, s_made, on_summed, ab_trans, last_made, qk_squared, qk_logged, qk_root, vt_ready, kt_ready, gam_ready, eg_ready, t_ready, p_ready, vn_ready, og_squared, on_logged, on_root, qkv_silu, z_silu, go_hi, ab_act, drained, conv_mac, gtab_ready, qn_ready, kn_ready, d_made, at_ready, pt_ready, xi_mul, x_init, t_upd, x_upd, r_made, vd_ready, mem_ready, og_normed, og_ready, go_ready, ab_dve, qg_ready, pt_masked, masks_made, g_stored, g_loaded) = [sem(n) for n in (
            "qk_summed", "v_trans", "k_trans", "kk_made", "qk_made", "x_trans", "p_made", "tt_made", "xx_made", "ks_made", "wr_made", "og_made", "s_made", "on_summed", "ab_trans", "last_made", "qk_squared", "qk_logged", "qk_root", "vt_ready", "kt_ready", "gam_ready", "eg_ready", "t_ready", "p_ready", "vn_ready", "og_squared", "on_logged", "on_root", "qkv_silu", "z_silu", "go_hi", "ab_act", "drained", "conv_mac", "gtab_ready", "qn_ready", "kn_ready", "d_made", "at_ready", "pt_ready", "xi_mul", "x_init", "t_upd", "x_upd", "r_made", "vd_ready", "mem_ready", "og_normed", "og_ready", "go_ready", "ab_dve", "qg_ready", "pt_masked", "masks_made", "g_stored", "g_loaded")]
        (ident_made, hg_const, f_scaled, f_sig, forget_made, key_made, f_logged, b_scanned, b_centered, b_ended,
         pos_ready, neg_ready, all_ready, end_ready, i_scaled, v_transposed, v_copied, k_transposed, k_copied, q_scaled,
         q_silu, g_scaled, g_silu, q_cen_ready, k_cen_ready, q_int_ready, k_end_ready, scores_made, probs_ready,
         ds_made, state_ready, o_made, o_squared, o_summed, o_logged, o_root, o_normed, o_gated, o_hi_ready, o_ready
         ) = [sem(n) for n in (
            "ident_made", "hg_const", "f_scaled", "f_sig", "forget_made", "key_made", "f_logged", "b_scanned", "b_centered",
            "b_ended", "pos_ready", "neg_ready", "all_ready", "end_ready", "i_scaled", "v_transposed", "v_copied",
            "k_transposed", "k_copied", "q_scaled", "q_silu", "g_scaled", "g_silu", "q_cen_ready", "k_cen_ready",
            "q_int_ready", "k_end_ready", "scores_made", "probs_ready", "ds_made", "state_ready", "o_made", "o_squared",
            "o_summed", "o_logged", "o_root", "o_normed", "o_gated", "o_hi_ready", "o_ready")]

        HG_CONST = 12
        N_CONST = 16
        N_HG = 32
        G_ROWS = 2 * (P // 16)
        if "gd" in kinds:
            g_rows = nc.dram_tensor("g_rows", [VH, TOK], f32, kind="Internal").ap()
        N_GD = 3 * 16
        N_MASKS = 3 + 3 * (2 * LEVELS + 1)

        def gd_unit(s, i, step, pair):
            u = first_unit[s] + 1 + 6 * step + i
            return (u, 12 * pair) if not isinstance(pair, int) else (u + 12 * pair, 0)

        block = ctx.enter_context(nc.Block())

        def count(u):
            return u[0] + u[1]

        def ahead(u, n):
            return (u[0] + n, u[1])

        def wait(eng, s, v):
            if not isinstance(v, int) or v > 0:
                eng.wait_ge(s, v)

        def post_gain(s, c):
            g = half_gains if kinds[s] == "ffn" else gains
            i = ((s // 3) * 6 + 2 * (s % 3) + 1) * KD + c
            return g[:, i:i + 1]

        def pre_gain(s, c):
            i = ((s // 3) * 6 + 2 * (s % 3)) * KD + c
            return gains[:, i:i + 1]

        @block.sync
        def _(sp):
            sp.dma_start(x[:], A["x"]).then_inc(x_loaded, 16)
            sp.dma_start(gains[:], A["gains"]).then_inc(const_loaded, 16)

            def load(u, src, n=UNIT):
                if u[0] >= RING or not isinstance(u[1], int):
                    wait(sp, lo_split, count(u) - RING + 1)
                sp.dma_start(raw[:, u[0] % RING, 0:n], src).then_inc(raw_loaded[u[0] % RING], 16)

            def ffn(s):
                u0 = first_unit[s]
                w_in = A["ffn_in"]
                w_out = A["ffn_out"]
                row0 = ffn_no[s] * 2 * KF

                def four(i, first=0):
                    for q in range(RING):
                        row = sp.snap(row0 + 4 * i + q) if not isinstance(i, int) else row0 + 4 * i + q
                        load((u0 + q, 4 * i) if not isinstance(i, int) else (u0 + q + 4 * i, 0),
                             w_in[bass.ds(row, 1), :, :].rearrange("a p n -> (a p) n"))
                four(0)
                with sp.Fori(1, 2 * KF // RING) as i:
                    four(i)
                out_loads(s, w_out, ffn_no[s] * KD)

            def out_loads(s, w_out, row0):
                cuts = CUTS[kinds[s]]
                n_u = len(cuts) - 1
                tiles = RING // n_u
                v0 = first_unit[s] + IN_UNITS[kinds[s]]
                with sp.Fori(0, KD // tiles) as i:
                    for t in range(tiles):
                        for q in range(n_u):
                            row = sp.snap(row0 + tiles * i + t)
                            a, b = cuts[q] * P, cuts[q + 1] * P
                            load((v0 + t * n_u + q, 4 * i), w_out[bass.ds(row, 1), :, a:b].rearrange("a p n -> (a p) n"), b - a)

            def hgrn2(s):
                for q in range(RING):
                    load((first_unit[s] + q, 0), A["hg_in"][q:q + 1, :, :].rearrange("a p n -> (a p) n"))
                wait(sp, sum_ready, 2 * s)
                sp.dma_start(bound_tmp[:, 0, :], A["hg_bounds"]).then_inc(hg_loaded, 16)
                sp.dma_start(hg_gain[:], A["hg_gain"]).then_inc(hg_loaded, 16)
                with sp.Fori(1, HEADS) as j:
                    for q in range(4):
                        row = sp.snap(4 * j + q)
                        load((first_unit[s] + q, 4 * j), A["hg_in"][bass.ds(row, 1), :, :].rearrange("a p n -> (a p) n"))
                out_loads(s, A["hg_out"], 0)

            def deltanet(s):
                def group(j, step, pair, tiles=range(6)):
                    for i in tiles:
                        row = sp.snap(6 * j + 1 + i) if not isinstance(j, int) else 6 * j + 1 + i
                        load(gd_unit(s, i, step, pair), A["gd_in"][bass.ds(row, 1), :, :].rearrange("a p n -> (a p) n"))

                def rows(j):
                    if isinstance(j, int):
                        wait(sp, qg_ready, 2 * j)
                    else:
                        first = sp.snap(2 * j)
                        sp.wait_ge(qg_ready, 2 * j)
                        j = None
                    src = g_rows[bass.ds(first, 2), :] if j is None else g_rows[2 * j:2 * j + 2, :]
                    sp.dma_start(g_bc[:], src.rearrange("(o h) t -> o h t", o=1).to_broadcast([P, 2, TOK])).then_inc(g_loaded, 16)

                load((first_unit[s], 0), A["gd_in"][0:1, :, :].rearrange("a p n -> (a p) n"))
                group(0, 0, 0, range(RING - 1))
                wait(sp, sum_ready, 2 * s)
                sp.dma_start(conv_w[:], A["gd_conv"]).then_inc(ab_loaded, 16)
                sp.dma_start(gd_gain[:], A["gd_gain"]).then_inc(ab_loaded, 16)
                sp.dma_start(gd_ab[:], A["gd_ab"]).then_inc(ab_loaded, 16)
                group(0, 0, 0, range(RING - 1, 6))
                sp.wait_ge(ab_dve, 5)
                sp.dma_start(g_rows, g_row_tile[32:AB, :]).then_inc(g_stored, 16)
                sp.wait_ge(g_stored, 16)
                rows(0)
                with sp.Fori(0, 3) as k:
                    for d in (1, 2):
                        group(2 * k + d, d, k)
                        rows(2 * k + d)
                group(7, 1, 3)
                rows(7)
                out_loads(s, A["gd_out"], 0)

            for s, kind in enumerate(kinds):
                {"ffn": ffn, "hg": hgrn2, "gd": deltanet}[kind](s)
            for c in range(KD):
                sp.wait_ge(x_ready, KD * (LAST - 1) + c + 1)
                sp.dma_start(out[:, c, :], x[:, c, :]).then_inc(stored, 16)
            sp.wait_ge(stored, 16 * KD)

        @block.scalar
        def _(act):
            def split(u):
                if u[0] >= RING or not isinstance(u[1], int):
                    wait(act, unit_used, count(u) - RING + 1)
                act.wait_ge(raw_loaded[u[0] % RING], 16 * (u[0] // RING + 1) + 4 * u[1])
                nc.scalar.activation(w_hi[:, u[0] % RING, :], raw[:, u[0] % RING, :], ACT.Copy).then_inc(hi_split, 1)

            def square(q, c, src):
                wait(act, acc_done, KD * q + c - 1)
                nc.scalar.activation(sq[:, c % 2, :], src, ACT.Square).then_inc(sq_done, 1)

            def root(q):
                act.wait_ge(sum_ready, q + 1)
                nc.scalar.activation(rms[:, q % 2, :], bank[4][:], ACT.Ln, bias=eps[:], scale=1.0 / D).then_inc(rms_logged, 1)
                act.wait_ge(rms_logged, q + 1)
                nc.scalar.activation(rms[:, q % 2, :], rms[:, q % 2, :], ACT.Exp, scale=-0.5).then_inc(rms_ready, 1)

            def pre(s):
                for c in range(KD):
                    if s == 0:
                        act.wait_ge(x_loaded, 16)
                        act.wait_ge(const_loaded, N_CONST)
                        act.wait_ge(const_made, 3)
                    else:
                        act.wait_ge(x_ready, KD * (s - 1) + c + 1)
                    nc.scalar.activation(h_hi[:, c, :], x[:, c, :], ACT.Copy, scale=pre_gain(s, c)).then_inc(h_hi_ready, 1)
                    square(2 * s, c, x[:, c, :])
                if s == 0:
                    act.preload_act_table_set("natural_log_exp_and_others")
                root(2 * s)

            def out_tile(s, c, b):
                act.wait_ge(unit_used, c[1])
                nc.scalar.activation(m[:, c[0], :], bank[b][:], ACT.Copy)

            def ffn(s):
                u0 = first_unit[s]
                n0 = ffn_no[s] * KF

                def pair(u, n, par):
                    act.wait_ge(gate_scaled, n0 + n + 1)
                    wait(act, act_mul, n0 + n)
                    nc.scalar.activation(silu, gate[:], ACT.Silu).then_inc(gate_silu, 1)
                    split(ahead(u, 4))
                    split(ahead(u, 5))
                    act.wait_ge(act_mul, n0 + n + 1)
                    nc.scalar.activation(act_hi[:, bass.ds(n, 1), :].rearrange("p a n -> p (a n)"), prod, ACT.Copy).then_inc(act_hi_ready, 1)

                pair((u0, 0), 0, 0)
                pair((u0 + 2, 0), 1, 1)
                with act.Fori(1, KF // 2) as i:
                    pair((u0, 4 * i), 2 * i, 0)
                    pair((u0 + 2, 4 * i), 2 * i + 1, 1)
                out_tiles(s)

            def out_tiles(s):
                n_u = len(CUTS[kinds[s]]) - 1
                tiles = RING // n_u
                v0 = first_unit[s] + IN_UNITS[kinds[s]]

                def four(i, last=False):
                    for t in range(max(tiles, 2)):
                        u = (v0 + t * n_u, 4 * i) if not isinstance(i, int) else (v0 + 4 * i + t * n_u, 0)
                        c = tiles * i + t
                        more = not last or t * n_u + RING < max(tiles, 2) * n_u
                        for q in range(n_u - 1):
                            if more:
                                split(ahead(u, 4 + q))
                        act.wait_ge(unit_used, count(u) + n_u)
                        wait(act, y_scaled, KD * s)
                        nc.scalar.activation(m[:, bass.ds(c, 1), :].rearrange("p a n -> p (a n)"), bank[t % 2][:], ACT.Copy).then_inc(m_copied, 1)
                        wait(act, acc_done, KD * (2 * s + 1) + c - 1)
                        nc.scalar.activation(sq[:, t % 2, :], bank[t % 2][:], ACT.Square).then_inc(sq_done, 1)
                        if more:
                            split(ahead(u, 3 + n_u))
                step = max(tiles, 2) // tiles
                n = KD // tiles
                act.preload_act_table_set("natural_log_exp_and_others")
                with act.Fori(0, n - step, step) as i:
                    four(i)
                four(n - step, s == LAST - 1)
                root(2 * s + 1)

            def hgrn2(s):
                u0 = first_unit[s]

                act.wait_ge(hg_const, 4)
                nc.scalar.activation(bound_tmp[:, 2, :], bound_tmp[:, 1, :], ACT.Exp).then_inc(hg_const, 1)

                def step(j, gemm, chain):
                    u = (u0, 4 * j) if not isinstance(j, int) else (u0 + 4 * j, 0)
                    if chain:
                        act.wait_ge(v_transposed, j)
                        nc.scalar.activation(v_tok[:].rearrange("p t v -> p (t v)"), bank[2][:], ACT.Copy).then_inc(v_copied, 1)
                    if gemm:
                        split(ahead(u, 4))
                        act.wait_ge(f_scaled, j + 1)
                        nc.scalar.activation(sig[:], f_in[:], ACT.Sigmoid).then_inc(f_sig, 1)
                        act.preload_act_table_set("natural_log_exp_and_others")
                        act.wait_ge(forget_made, j + 1)
                        wait(act, b_ended, j)
                        nc.scalar.activation(logf[:], forget[:], ACT.Ln).then_inc(f_logged, 1)
                        act.wait_ge(b_centered, j + 1)
                        wait(act, q_cen_ready, j)
                        nc.scalar.activation(e_pos[:], b_mid[:], ACT.Exp).then_inc(pos_ready, 1)
                        nc.scalar.activation(e_neg[:], b_mid[:], ACT.Exp, scale=-1.0).then_inc(neg_ready, 1)
                        wait(act, state_ready, (NCH - 1) * j)
                        wait(act, q_int_ready, j)
                        nc.scalar.activation(e_all[:], b[:], ACT.Exp).then_inc(all_ready, 1)
                        act.wait_ge(b_ended, j + 1)
                        nc.scalar.activation(e_end[:], b_end[:], ACT.Exp).then_inc(end_ready, 1)
                        split(ahead(u, 5))
                    if chain:
                        act.wait_ge(o_made, j)
                        nc.scalar.activation(osq[:], bank[2][:], ACT.Square).then_inc(o_squared, 1)
                    if gemm:
                        split(ahead(u, 6))
                    if chain:
                        act.wait_ge(o_summed, j)
                        wait(act, o_normed, j - 1)
                        nc.scalar.activation(o_rms[:], bank[3][:], ACT.Ln, bias=eps[:], scale=1.0 / P).then_inc(o_logged, 1)
                        act.wait_ge(o_logged, j)
                        nc.scalar.activation(o_rms[:], o_rms[:], ACT.Exp, scale=-0.5).then_inc(o_root, 1)
                        act.wait_ge(o_gated, j)
                        nc.scalar.activation(o_hi[:, bass.ds(j - 1, 1), :].rearrange("p a n -> p (a n)"), o_fm[:], ACT.Copy).then_inc(o_hi_ready, 1)
                    if gemm:
                        act.wait_ge(q_scaled, j + 1)
                        nc.scalar.activation(q_act[:], q_in[:], ACT.Silu).then_inc(q_silu, 1)
                        split(ahead(u, 7))
                        act.wait_ge(g_scaled, j + 1)
                        nc.scalar.activation(g_act[:], g_in[:], ACT.Silu).then_inc(g_silu, 1)
                step(0, True, False)
                with act.Fori(1, HEADS) as j:
                    step(j, True, True)
                step(HEADS, False, True)
                out_tiles(s)

            def deltanet(s):
                def copy(dst, src):
                    return nc.scalar.activation(dst, src, ACT.Copy)

                def conv_silu(j, i):
                    act.wait_ge(conv_mac, 4 * (4 * j + i + 1))
                    if i == 0:
                        wait(act, qn_ready, j)
                    elif i == 1:
                        wait(act, kn_ready, j)
                    else:
                        wait(act, v_trans, 2 * (j - 1) + i - 1)
                    dst = (q_a[:], k_a[:], v_a[:, 0, :], v_a[:, 1, :])[i]
                    nc.scalar.activation(dst, (gate, up)[i % 2][:], ACT.Silu).then_inc(qkv_silu, 1)

                def z_out(j, e):
                    act.wait_ge(drained, 6 * (j + 1) + e)
                    wait(act, og_ready, 2 * (j - 1) + e + 1)
                    nc.scalar.activation(z_a[:, e, :], (gate, up)[e][:], ACT.Silu).then_inc(z_silu, 1)

                def betas():
                    act.wait_ge(ab_dve, 1)
                    act.wait_ge(drained, 1)
                    nc.scalar.activation(g_row_tile[0:VH, :], ab_in[0:VH, :], ACT.Sigmoid).then_inc(ab_act, 1)
                    act.preload_act_table_set("natural_log_exp_and_others")
                    act.wait_ge(ab_dve, 2)
                    nc.scalar.activation(ab_exp[32:AB, :], ab_in[32:AB, :], ACT.Abs).then_inc(ab_act, 1)
                    act.wait_ge(ab_act, 2)
                    nc.scalar.activation(ab_exp[32:AB, :], ab_exp[32:AB, :], ACT.Exp, scale=-1.0).then_inc(ab_act, 1)
                    act.wait_ge(ab_act, 3)
                    nc.scalar.activation(ab_exp[32:AB, :], ab_exp[32:AB, :], ACT.Ln, bias=ones[32:AB, 0:1]).then_inc(ab_act, 1)
                    nc.scalar.activation(ea[32:AB, :], gd_ab[32:AB, 1:2], ACT.Exp).then_inc(ab_act, 1)
                    act.wait_ge(ab_dve, 6)
                    nc.scalar.activation(tab[:, 1, :, :], tab[:, 0, :, :], ACT.Exp).then_inc(ab_act, 1)
                    act.wait_ge(last_made, 1)
                    nc.scalar.activation(tab[:, 4, :, :], bank[7][:, 0:NT * VH].rearrange("p (t h) -> p t h", h=VH), ACT.Exp).then_inc(ab_act, 1)
                    act.wait_ge(ab_dve, 9)
                    nc.scalar.activation(tab[:, 3, :, :], tab[:, 3, :, :], ACT.Exp).then_inc(ab_act, 1)

                def step(j, d, pair, gemm, chain):
                    g = j - 1

                    def done(i):
                        if gemm:
                            split(ahead(gd_unit(s, i, d, pair), 4))

                    if chain:
                        wait(act, og_normed, 2 * g)
                        act.wait_ge(qkv_silu, 4 * j)
                        nc.scalar.activation(y[:, 0, :], q_a[:], ACT.Square).then_inc(qk_squared, 1)
                        nc.scalar.activation(y[:, 1, :], k_a[:], ACT.Square).then_inc(qk_squared, 1)
                        act.preload_act_table_set("natural_log_exp_and_others")
                        for e in range(2):
                            act.wait_ge(qk_summed, 2 * g + e + 1)
                            nc.scalar.activation(y[:, e, :], bank[2 + e][:], ACT.Ln, bias=eps[:]).then_inc(qk_logged, 1)
                            act.wait_ge(qk_logged, 2 * g + e + 1)
                            nc.scalar.activation(y[:, e, :], y[:, e, :], ACT.Exp, scale=-0.5).then_inc(qk_root, 1)
                        for e in range(2):
                            act.wait_ge(d_made, 2 * g + e + 1)
                            nc.scalar.activation(attn[:, e, :, :], attn[:, e, :, :], ACT.Exp).then_inc(gam_ready, 1)
                        nc.scalar.activation(g_bc[:], g_bc[:], ACT.Exp).then_inc(eg_ready, 1)
                        for e in range(2):
                            act.wait_ge(v_trans, 2 * g + e + 1)
                            copy(vt[:, e, :, :], bank[4 + e][:].rearrange("p (t v) -> p t v", v=P)).then_inc(vt_ready, 1)
                        act.wait_ge(k_trans, g + 1)
                        copy(kt[:], bank[6][:]).then_inc(kt_ready, 1)
                    if gemm:
                        done(0)
                    if chain:
                        for e in range(2):
                            act.wait_ge(x_trans, 2 * g + e + 1)
                            wait(act, p_made, 12 * g)
                            copy(inv[:, e, :, :], bank[3 + e][:].rearrange("p (t v) -> p t v", v=P)).then_inc(t_ready, 1)
                    if gemm:
                        conv_silu(j, 0)
                    for l in range(1, LEVELS):
                        if chain:
                            for e in range(2):
                                act.wait_ge(p_made, 12 * g + 2 * (l - 1) + e + 1)
                                copy(prod_at[:, e, :, :], bank[5 + e][:].rearrange("p (t v) -> p t v", v=P)).then_inc(p_ready, 1)
                        if gemm and l == 2:
                            done(1)
                        if gemm and l == 3:
                            conv_silu(j, 1)
                        if gemm and l == 5:
                            done(2)
                        if gemm and l == 6:
                            conv_silu(j, 2)
                    if gemm:
                        done(3)
                    for t in range(NT):
                        if gemm and t == 3:
                            conv_silu(j, 3)
                            done(4)
                    if chain:
                        for e in range(2):
                            act.wait_ge(og_made, 2 * g + e + 1)
                            nc.scalar.activation(y[:, e, :], bank[(7, 2)[e]][:], ACT.Square).then_inc(og_squared, 1)
                        act.preload_act_table_set("natural_log_exp_and_others")
                        for e in range(2):
                            act.wait_ge(on_summed, 2 * g + e + 1)
                            nc.scalar.activation(y[:, e, :], bank[5 + e][:], ACT.Ln, bias=eps[:], scale=1.0 / P).then_inc(on_logged, 1)
                            act.wait_ge(on_logged, 2 * g + e + 1)
                            nc.scalar.activation(y[:, e, :], y[:, e, :], ACT.Exp, scale=-0.5).then_inc(on_root, 1)
                    if gemm:
                        z_out(j, 0)
                        done(5)
                        z_out(j, 1)

                split((first_unit[s] + RING, 0))
                act.wait_ge(ab_loaded, N_GD)
                betas()
                for i in range(4):
                    conv_silu(0, i)
                    if i < 3:
                        split(ahead((first_unit[s] + 1 + i, 0), 4))
                for i in (3, 4):
                    split(ahead((first_unit[s] + 1 + i, 0), 4))
                z_out(0, 0)
                split(ahead((first_unit[s] + 6, 0), 4))
                z_out(0, 1)
                with act.Fori(0, 3) as k:
                    step(2 * k + 1, 1, k, True, True)
                    step(2 * k + 2, 2, k, True, True)
                step(7, 1, 3, True, True)
                step(8, 2, 3, False, True)
                for k in range(VH):
                    act.wait_ge(og_ready, k + 1)
                    dst = h_hi[:, k, :] if k < KD else go_hi_b[:, k - KD, :]
                    copy(dst, gd_o[:, k, :]).then_inc(go_hi, 1)
                out_tiles(s)

            for u in range(RING):
                split((u, 0))
            for s, kind in enumerate(kinds):
                pre(s)
                {"ffn": ffn, "hg": hgrn2, "gd": deltanet}[kind](s)

        @block.vector
        def _(dve):
            def split(u):
                dve.wait_ge(hi_split, count(u) + 1)
                r = u[0] % RING
                nc.vector.tensor_tensor(w_lo[:, r, :], raw[:, r, :], w_hi[:, r, :].bitcast(f32), ALU.subtract).then_inc(lo_split, 1)

            def low(s, c):
                dve.wait_ge(h_hi_ready, KD * s + c + 1)
                nc.vector.scalar_tensor_tensor(out=h_lo[:, c, :], in0=x[:, c, :], scalar=pre_gain(s, c),
                                               in1=h_hi[:, c, :].bitcast(f32), op0=ALU.mult, op1=ALU.subtract).then_inc(h_ready, 1)

            def boundary(s):
                dve.wait_ge(rms_ready, 2 * s)
                dve.wait_ge(m_copied, KD * s)

                def scale(c):
                    wait(dve, x_ready, KD * (s - 1) + c - 1)
                    nc.vector.scalar_tensor_tensor(out=y[:, c % 2, :], in0=m[:, c, :], scalar=post_gain(s - 1, c),
                                                   in1=rms[:, 1, :], op0=ALU.mult, op1=ALU.mult).then_inc(y_scaled, 1)

                def add(c):
                    dve.wait_ge(y_scaled, KD * (s - 1) + c + 1)
                    nc.vector.tensor_tensor(x[:, c, :], x[:, c, :], y[:, c % 2, :], ALU.add).then_inc(x_ready, 1)
                scale(0)
                for c in range(KD):
                    if c + 1 < KD:
                        scale(c + 1)
                    add(c)
                    if c and s < LAST:
                        low(s, c - 1)
                if s < LAST:
                    low(s, KD - 1)

            def ffn(s):
                u0 = first_unit[s]
                n0 = ffn_no[s] * KF
                dve.wait_ge(rms_ready, 2 * s + 1)

                def pair(u, n, par):
                    dve.wait_ge(unit_used, count(u) + 1)
                    wait(dve, gate_silu, n0 + n)
                    nc.vector.tensor_tensor(gate[:], bank[2 * par][:], rms[:, 0, :], ALU.mult).then_inc(gate_scaled, 1)
                    dve.wait_ge(unit_used, count(u) + 2)
                    wait(dve, act_mul, n0 + n)
                    nc.vector.tensor_tensor(up[:], bank[2 * par + 1][:], rms[:, 0, :], ALU.mult).then_inc(up_scaled, 1)
                    split(ahead(u, 4))
                    split(ahead(u, 5))
                    dve.wait_ge(act_hi_ready, n0 + n + 1)
                    nc.vector.tensor_tensor(act_lo[:, bass.ds(n, 1), :].rearrange("p a n -> p (a n)"), prod,
                                            act_hi[:, bass.ds(n, 1), :].rearrange("p a n -> p (a n)").bitcast(f32), ALU.subtract).then_inc(act_ready, 1)
                pair((u0, 0), 0, 0)
                pair((u0 + 2, 0), 1, 1)
                with dve.Fori(1, KF // 2) as i:
                    pair((u0, 4 * i), 2 * i, 0)
                    pair((u0 + 2, 4 * i), 2 * i + 1, 1)
                out_splits(s)

            def out_splits(s):
                kind = kinds[s]
                v0 = first_unit[s] + IN_UNITS[kind]
                n_out = N_UNITS[kind] - IN_UNITS[kind]
                with dve.Fori(0, n_out if s < LAST - 1 else n_out - RING, RING) as i:
                    for q in range(RING):
                        split((v0 + RING + q, i))

            def by_chunk(t):
                return t[:].rearrange("p (n c) -> p n c", c=CH)

            def hgrn2(s):
                TT = nc.vector.tensor_tensor
                u0 = first_unit[s]
                dve.wait_ge(hg_loaded, N_HG)
                TT(bound_tmp[:, 1, :], bound_tmp[:, 0, :], bound_tmp[:, 0, :], ALU.subtract).then_inc(hg_const, 1)
                nc.vector.memset(scan_keep[:], 1.0).then_inc(hg_const, 1)
                nc.vector.memset(probs[:], 0.0).then_inc(hg_const, 1)
                dve.wait_ge(hg_const, 3)
                nc.vector.memset(by_chunk(scan_keep)[:, :, 0:1], 0.0).then_inc(hg_const, 1)
                dve.wait_ge(hg_const, 5)
                nc.vector.reciprocal(bound_tmp[:, 1, :], bound_tmp[:, 2, :]).then_inc(hg_const, 1)
                dve.wait_ge(hg_const, 6)
                TT(bound_tmp[:, 0, :], bound_tmp[:, 1, :], bound_tmp[:, 2, :], ALU.mult).then_inc(hg_const, 1)
                dve.wait_ge(hg_const, 7)
                TT(bound[:], bound_tmp[:, 0, :], bound_tmp[:, 0, :], ALU.subtract).then_inc(hg_const, 1)
                dve.wait_ge(hg_const, 8)
                nc.vector.tensor_scalar(bound_rest[:], bound[:], -1.0, 1.0, ALU.mult, ALU.add).then_inc(hg_const, 1)
                dve.wait_ge(ident_made, 4)
                nc.vector.memset(causal[:], 0.0).then_inc(hg_const, 1)
                dve.wait_ge(hg_const, 10)
                nc.vector.tensor_copy(causal[0:CH, 0:CH], upper[0:CH, 0:CH]).then_inc(hg_const, 1)
                nc.vector.tensor_copy(causal[CH:P, CH:P], upper[CH:P, CH:P]).then_inc(hg_const, 1)
                dve.wait_ge(hg_const, 12)
                dve.wait_ge(rms_ready, 2 * s + 1)
                r = rms[:, 0, :]

                def step(j, gemm, chain):
                    u = (u0, 4 * j) if not isinstance(j, int) else (u0 + 4 * j, 0)
                    tb = (0, 1, 2, 3) if isinstance(j, int) else (0, 1, 0, 1)
                    TT = nc.vector.tensor_tensor
                    if chain:
                        dve.wait_ge(k_transposed, j)
                        wait(dve, ds_made, j - 1)
                        nc.vector.tensor_copy(k_tok[:].rearrange("p t v -> p (t v)"), bank[3][:]).then_inc(k_copied, 1)
                    if gemm:
                        dve.wait_ge(unit_used, count(u) + 1)
                        wait(dve, f_sig, j)
                        if chain:
                            wait(dve, o_made, j - 1)
                            dve.wait_ge(scores_made, j)
                        TT(f_in[:], bank[tb[0]][:], r, ALU.mult).then_inc(f_scaled, 1)
                    elif chain:
                        wait(dve, o_made, j - 1)
                        dve.wait_ge(scores_made, j)
                    if chain:
                        nc.vector.copy_predicated(probs[:], causal[:].bitcast(mybir.dt.uint32).unsqueeze(1).to_broadcast([P, NT, P]),
                                                  bank[5][:].rearrange("p (t c) -> p t c", c=P)).then_inc(probs_ready, 1)
                        dve.wait_ge(ds_made, j)
                        nc.vector.tensor_copy(state[:, 0, :], bank[6][:, 0:P]).then_inc(state_ready, 1)
                        for n in range(1, NCH - 1):
                            dve.wait_ge(state_ready, (NCH - 1) * (j - 1) + n)
                            nc.vector.scalar_tensor_tensor(out=state[:, n, :], in0=state[:, n - 1, :], scalar=e_all[:, n * CH + CH - 1:n * CH + CH],
                                                           in1=bank[6 + n % 2][:, n // 2 * P:(n // 2 + 1) * P],
                                                           op0=ALU.mult, op1=ALU.add).then_inc(state_ready, 1)
                    if gemm:
                        dve.wait_ge(f_sig, j + 1)
                        nc.vector.tensor_scalar(forget[:], sig[:], bound_rest[:, bass.ds(j, 1)], bound[:, bass.ds(j, 1)], ALU.mult, ALU.add).then_inc(forget_made, 1)
                        dve.wait_ge(forget_made, j + 1)
                        wait(dve, k_end_ready, j)
                        nc.vector.tensor_scalar(key[:], forget[:], -1.0, 1.0, ALU.mult, ALU.add).then_inc(key_made, 1)
                        split(ahead(u, 4))
                        dve.wait_ge(f_logged, j + 1)
                        wait(dve, all_ready, j)
                        nc.vector.tensor_tensor_scan(b[:], scan_keep[:], logf[:], 0.0, ALU.mult, ALU.add).then_inc(b_scanned, 1)
                        dve.wait_ge(b_scanned, j + 1)
                        wait(dve, neg_ready, j)
                        TT(by_chunk(b_mid), by_chunk(b), by_chunk(b)[:, :, CH // 2:CH // 2 + 1].to_broadcast([P, NCH, CH]), ALU.subtract).then_inc(b_centered, 1)
                        wait(dve, end_ready, j)
                        TT(by_chunk(b_end), by_chunk(b)[:, :, CH - 1:CH].to_broadcast([P, NCH, CH]), by_chunk(b), ALU.subtract).then_inc(b_ended, 1)
                        dve.wait_ge(unit_used, count(u) + 2)
                        wait(dve, v_transposed, j)
                        TT(v_fm[:], bank[tb[1]][:], r, ALU.mult).then_inc(i_scaled, 1)
                        split(ahead(u, 5))
                        dve.wait_ge(neg_ready, j + 1)
                        TT(k_cen[:], key[:], e_neg[:], ALU.mult).then_inc(k_cen_ready, 1)
                        split(ahead(u, 6))
                    if chain:
                        dve.wait_ge(o_root, j)
                        wait(dve, o_gated, j - 1)
                        nc.vector.scalar_tensor_tensor(out=osq[:], in0=bank[2][:], scalar=hg_gain[:], in1=o_rms[:], op0=ALU.mult, op1=ALU.mult).then_inc(o_normed, 1)
                        dve.wait_ge(o_normed, j)
                        wait(dve, o_ready, j - 1)
                        dve.wait_ge(g_silu, j)
                        TT(o_fm[:], osq[:], g_act[:], ALU.mult).then_inc(o_gated, 1)
                    if gemm:
                        dve.wait_ge(unit_used, count(u) + 3)
                        wait(dve, q_silu, j)
                        TT(q_in[:], bank[tb[2]][:], r, ALU.mult).then_inc(q_scaled, 1)
                    if chain:
                        dve.wait_ge(o_hi_ready, j)
                        TT(o_lo[:, bass.ds(j - 1, 1), :].rearrange("p a n -> p (a n)"), o_fm[:],
                           o_hi[:, bass.ds(j - 1, 1), :].rearrange("p a n -> p (a n)").bitcast(f32), ALU.subtract).then_inc(o_ready, 1)
                    if gemm:
                        dve.wait_ge(q_silu, j + 1)
                        TT(q_cen[:], q_act[:], e_pos[:], ALU.mult).then_inc(q_cen_ready, 1)
                        split(ahead(u, 7))
                        dve.wait_ge(unit_used, count(u) + 4)
                        wait(dve, g_silu, j)
                        TT(g_in[:], bank[tb[3]][:], r, ALU.mult).then_inc(g_scaled, 1)
                step(0, True, False)
                with dve.Fori(1, HEADS) as j:
                    step(j, True, True)
                step(HEADS, False, True)
                out_splits(s)

            def deltanet(s):
                TT = nc.vector.tensor_tensor
                r = rms[:, 0, :]

                def drain(j, i, b, d=None, pair=None):
                    u = gd_unit(s, i, d, pair)
                    dve.wait_ge(unit_used, count(u) + 1)
                    if i < 4:
                        wait(dve, conv_mac, 4 * (4 * j + i))
                        TT(pre[:, TAPS - 1:], bank[b][:], r, ALU.mult).then_inc(drained, 1)
                    else:
                        dve.wait_ge(qkv_silu, 4 * j + i - 1)
                        TT((gate, up)[i % 2][:], bank[b][:], r, ALU.mult).then_inc(drained, 1)

                def mac(j, i, tap):
                    dst = (gate, up)[i % 2][:]
                    w = conv_w[:, bass.ds(j, 1), i, tap:tap + 1].rearrange("p a b -> p (a b)")
                    if tap == 0:
                        dve.wait_ge(drained, 2 + i + (6 * j if not isinstance(j, int) else 6 * j))
                        if i < 2:
                            wait(dve, z_silu, 2 * (j - 1) + i + 1)
                        else:
                            dve.wait_ge(qkv_silu, 4 * j + i - 1)
                        nc.vector.tensor_scalar(dst, pre[:, 0:TOK], w, None, ALU.mult).then_inc(conv_mac, 1)
                    else:
                        dve.wait_ge(conv_mac, 4 * (4 * j + i) + tap)
                        nc.vector.scalar_tensor_tensor(out=dst, in0=pre[:, tap:tap + TOK], scalar=w, in1=dst,
                                                       op0=ALU.mult, op1=ALU.add).then_inc(conv_mac, 1)

                def lo(i, d, pair):
                    split(ahead(gd_unit(s, i, d, pair), 4))

                def betas():
                    nc.vector.memset(inv[:], 0.0).then_inc(ab_dve, 1)
                    nc.vector.memset(keep_rows, 1.0)
                    dve.wait_ge(rms_ready, 2 * s + 1)
                    dve.wait_ge(ab_dve, 1)
                    TT(ab_in, bank[0][0:AB, :], rms[0:AB, 0, :], ALU.mult).then_inc(drained, 1)
                    dve.wait_ge(drained, 1)
                    nc.vector.memset(keep_rows.rearrange("p (t c) -> p t c", c=P)[:, :, 0:1], 0.0)
                    nc.vector.tensor_scalar(ab_in[32:AB, :], ab_in[32:AB, :], gd_ab[32:AB, 0:1], None, ALU.add).then_inc(ab_dve, 1)
                    dve.wait_ge(ab_act, 5)
                    nc.vector.scalar_tensor_tensor(out=g_step[32:AB, :], in0=ab_in[32:AB, :], scalar=0.0, in1=ab_exp[32:AB, :],
                                                   op0=ALU.max, op1=ALU.add).then_inc(ab_dve, 1)
                    dve.wait_ge(ab_dve, 3)
                    nc.vector.tensor_scalar(g_step[32:AB, :], g_step[32:AB, :], ea[32:AB, :], -1.0, ALU.mult, ALU.mult).then_inc(ab_dve, 1)
                    dve.wait_ge(ab_dve, 4)
                    nc.vector.tensor_tensor_scan(g_row_tile[32:AB, :], keep_rows[32:AB, :], g_step[32:AB, :], 0.0, ALU.mult, ALU.add).then_inc(ab_dve, 1)
                    dve.wait_ge(ab_trans, 1)
                    src = bank[6][:, 0:NT * AB].rearrange("p (t h) -> p t h", h=AB)
                    nc.vector.tensor_copy(tab[:, 0, :, :], src[:, :, 32:AB]).then_inc(ab_dve, 1)
                    nc.vector.tensor_copy(tab[:, 2, :, :], src[:, :, 0:VH])
                    dve.wait_ge(ab_act, 6)
                    nc.vector.tensor_scalar(tab[:, 1, :, :], tab[:, 1, :, :], -1.0, None, ALU.mult).then_inc(ab_dve, 1)
                    dve.wait_ge(ab_dve, 7)
                    nc.vector.tensor_scalar(tab[:, 5, :, :], tab[:, 2, :, :], -1.0, None, ALU.mult).then_inc(ab_dve, 1)
                    dve.wait_ge(ab_act, 7)
                    dve.wait_ge(last_made, 1)
                    TT(tab[:, 3, :, :], bank[7][:, 0:NT * VH].rearrange("p (t h) -> p t h", h=VH), tab[:, 0, :, :], ALU.subtract).then_inc(ab_dve, 1)
                    dve.wait_ge(ab_act, 8)
                    TT(tab[:, 3, :, :], tab[:, 3, :, :], tab[:, 2, :, :], ALU.mult).then_inc(ab_dve, 1)
                    dve.wait_ge(ab_dve, 10)

                def flat(x, e):
                    return x[:, e, :, :].rearrange("p t c -> p (t c)")

                def as_tiles(b):
                    return b[:].rearrange("p (t c) -> p t c", c=P)

                def wide(mask):
                    return mask.unsqueeze(1).to_broadcast([P, NT, P])

                def step(j, d, pair, gemm, chain):
                    g = j - 1
                    if chain:
                        wait(dve, vd_ready, 8 * g)
                        wait(dve, mem_ready, 6 * g)
                        wait(dve, vn_ready, 8 * g)
                        nc.vector.tensor_scalar(gtab[:], tab[:, :, :, bass.ds(2 * g, 2)], 1.0, None, ALU.mult).then_inc(gtab_ready, 1)
                        dve.wait_ge(gtab_ready, g + 1)
                        dve.wait_ge(g_loaded, 16 * (g + 1))
                        wait(dve, og_made, 2 * g)
                        for e in range(2):
                            for t in range(NT):
                                ins = nc.vector.tensor_scalar(attn[:, e, t, :], g_bc[:, e, t * P:(t + 1) * P], gtab[:, 0, t, e:e + 1], 0.0, ALU.subtract, ALU.min)
                            ins.then_inc(d_made, 1)
                        dve.wait_ge(qk_root, 2 * g + 1)
                        wait(dve, og_made, 2 * g)
                        nc.vector.scalar_tensor_tensor(out=qn, in0=q_a[:], scalar=float(P) ** -0.5, in1=y[:, 0, :], op0=ALU.mult, op1=ALU.mult).then_inc(qn_ready, 1)
                        dve.wait_ge(qk_root, 2 * g + 2)
                        TT(kn, k_a[:], y[:, 1, :], ALU.mult).then_inc(kn_ready, 1)
                        dve.wait_ge(kk_made, g + 1)
                        wait(dve, p_made, 12 * g)
                        for e in range(2):
                            dve.wait_ge(gam_ready, 2 * g + e + 1)
                            for t in range(NT):
                                ins = nc.vector.scalar_tensor_tensor(out=neg_at[:, e, t, :], in0=bank[7][:, t * P:(t + 1) * P], scalar=gtab[:, 5, t, e:e + 1],
                                                                     in1=attn[:, e, t, :], op0=ALU.mult, op1=ALU.mult)
                            ins.then_inc(at_ready, 1)
                            dve.wait_ge(at_ready, 2 * g + e + 1)
                            wait(dve, wr_made, 8 * g)
                            TT(inv_t[:, e, :, :], neg_at[:, e, :, :], wide(pair_mask[:]), ALU.mult).then_inc(xi_mul, 1)
                            dve.wait_ge(xi_mul, 2 * g + e + 1)
                            TT(inv_t[:, e, :, :], inv_t[:, e, :, :], wide(ident[:]), ALU.add).then_inc(x_init, 1)
                        dve.wait_ge(qk_made, g + 1)
                        for e in range(2):
                            TT(attn[:, e, :, :], attn[:, e, :, :], as_tiles(bank[2]), ALU.mult).then_inc(pt_ready, 1)
                    if gemm:
                        drain(j, 0, 0, d, pair)
                        for tap in range(TAPS):
                            mac(j, 0, tap)
                        lo(0, d, pair)
                    for l in range(1, LEVELS):
                        if chain:
                            last = l == LEVELS - 1
                            if not last:
                                dve.wait_ge(tt_made, 10 * g + 2 * l)
                                dve.wait_ge(x_init, 2 * g + 2)
                            dve.wait_ge(xx_made, 12 * g + 2 * l)
                            dve.wait_ge(t_ready, 2 * g + 2)
                            nc.vector.memset(spare[:], 0.0).then_inc(x_gate, 1)
                            for e in range(2):
                                if not last:
                                    nc.vector.copy_predicated(inv[:, e, :, :], wide(low_mask[:, l, :]), as_tiles(bank[(7, 2)[e]])).then_inc(t_upd, 1)
                            for e in range(2):
                                nc.vector.copy_predicated(inv_t[:, e, :, :], wide(up_mask[:, l, :]), as_tiles(bank[3 + e])).then_inc(x_upd, 1)
                        if gemm and l == 2:
                            drain(j, 1, 1, d, pair)
                            for tap in range(TAPS):
                                mac(j, 1, tap)
                            lo(1, d, pair)
                        if gemm and l == 5:
                            drain(j, 2, 0, d, pair)
                            for tap in range(TAPS):
                                mac(j, 2, tap)
                            lo(2, d, pair)
                    for t in range(NT):
                        if chain:
                            if t:
                                for e in range(2):
                                    dve.wait_ge(ks_made, 6 * g + 2 * (t - 1) + e + 1)
                                    dve.wait_ge(vt_ready, 2 * g + e + 1)
                                    nc.vector.scalar_tensor_tensor(out=resid_v[:, e, :], in0=bank[3 + e][:, 0:P], scalar=gtab[:, 1, t, e:e + 1],
                                                                   in1=vt[:, e, t, :], op0=ALU.mult, op1=ALU.add).then_inc(r_made, 1)
                            for e in range(2):
                                dve.wait_ge(wr_made, 8 * g + 2 * t + e + 1)
                                if t == 0:
                                    wait(dve, s_made, 6 * g)
                                nc.vector.tensor_scalar(v_dec[:, e, :], bank[5 + e][:, 0:P], gtab[:, 3, t, e:e + 1], None, ALU.mult).then_inc(vd_ready, 1)
                                nc.vector.tensor_scalar(v_new[:, e, :], bank[5 + e][:, 0:P], gtab[:, 2, t, e:e + 1], None, ALU.mult).then_inc(vn_ready, 1)
                        if gemm and t == 1:
                            drain(j, 3, 1, d, pair)
                        for tap in ((), (0,), (1,), (2, 3))[t] if gemm else ():
                            mac(j, 3, tap)
                        if chain and t < NT - 1:
                            for e in range(2):
                                dve.wait_ge(s_made, 6 * g + 2 * t + e + 1)
                                if t == 0:
                                    wait(dve, og_made, 2 * g)
                                    nc.vector.tensor_scalar(mem[:, e, 1, :], bank[3 + e][:, 0:P], 1.0, None, ALU.mult).then_inc(mem_ready, 1)
                                else:
                                    dve.wait_ge(mem_ready, 6 * g + 2 * t + e - 1)
                                    nc.vector.scalar_tensor_tensor(out=mem[:, e, (t + 1) % 2, :], in0=mem[:, e, t % 2, :], scalar=gtab[:, 4, t, e:e + 1],
                                                                   in1=bank[3 + e][:, 0:P], op0=ALU.mult, op1=ALU.add).then_inc(mem_ready, 1)
                    if gemm:
                        lo(3, d, pair)
                        drain(j, 4, 0, d, pair)
                    if chain:
                        for e in range(2):
                            dve.wait_ge(on_root, 2 * g + e + 1)
                            nc.vector.scalar_tensor_tensor(out=y[:, e, :], in0=bank[(7, 2)[e]][:], scalar=gd_gain[:], in1=y[:, e, :],
                                                           op0=ALU.mult, op1=ALU.mult).then_inc(og_normed, 1)
                            dve.wait_ge(og_normed, 2 * g + e + 1)
                            dve.wait_ge(z_silu, 2 * g + e + 1)
                            TT(gd_o[:, bass.ds(2 * g + e, 1), :].rearrange("p a n -> p (a n)"), y[:, e, :], z_a[:, e, :], ALU.mult).then_inc(og_ready, 1)
                    if gemm:
                        lo(4, d, pair)
                        drain(j, 5, 1, d, pair)
                        lo(5, d, pair)

                dve.wait_ge(ab_loaded, N_GD)
                nc.vector.memset(pre[:, 0:TAPS - 1], 0.0)
                split((first_unit[s] + RING, 0))
                betas()
                for i in range(4):
                    drain(0, i, (1, 2, 3, 0)[i], 0, 0)
                    for tap in range(TAPS):
                        mac(0, i, tap)
                    if i < 3:
                        lo(i, 0, 0)
                lo(3, 0, 0)
                drain(0, 4, 1, 0, 0)
                lo(4, 0, 0)
                drain(0, 5, 0, 0, 0)
                lo(5, 0, 0)
                dve.wait_ge(masks_made, N_MASKS)
                with dve.Fori(0, 3) as k:
                    step(2 * k + 1, 1, k, True, True)
                    step(2 * k + 2, 2, k, True, True)
                step(7, 1, 3, True, True)
                step(8, 2, 3, False, True)
                dve.wait_ge(og_ready, VH)
                for k in range(VH):
                    dve.wait_ge(go_hi, k + 1)
                    dst, hi = (go_lo_a[:, k, :], h_hi[:, k, :]) if k < KD else (go_lo_b[:, k - KD, :], go_hi_b[:, k - KD, :])
                    TT(dst, gd_o[:, k, :], hi.bitcast(f32), ALU.subtract).then_inc(go_ready, 1)
                out_splits(s)

            nc.vector.memset(ones[:], 1.0).then_inc(const_made, 1)
            nc.vector.memset(eps[:], 1e-6).then_inc(const_made, 1)
            dve.wait_ge(const_loaded, N_CONST)
            nc.vector.tensor_scalar(half_gains[:], gains[:], 0.5, None, ALU.mult).then_inc(const_made, 1)
            dve.wait_ge(const_made, 3)
            for u in range(RING):
                split((u, 0))
            dve.wait_ge(x_loaded, 16)
            for c in range(KD):
                low(0, c)
            for s, kind in enumerate(kinds):
                {"ffn": ffn, "hg": hgrn2, "gd": deltanet}[kind](s)
                boundary(s + 1)

        @block.gpsimd
        def _(pool):
            def total(q, c, par, first=False):
                pool.wait_ge(sq_done, KD * q + c + 1)
                if first:
                    wait(pool, sum_ready, q)
                    nc.gpsimd.tensor_copy(acc[:], sq[:, par, :]).then_inc(acc_done, 1)
                else:
                    pool.wait_ge(acc_done, KD * q + c)
                    nc.gpsimd.tensor_tensor(acc[:], acc[:], sq[:, par, :], ALU.add).then_inc(acc_done, 1)

            def sum8(q):
                total(q, 0, 0, True)
                total(q, 1, 1)
                with pool.Fori(2, KD, 2) as c:
                    total(q, c, 0)
                    total(q, c + 1, 1)

            def ffn(s):
                n0 = ffn_no[s] * KF
                with pool.Fori(0, KF) as n:
                    pool.wait_ge(gate_silu, n0 + n + 1)
                    pool.wait_ge(up_scaled, n0 + n + 1)
                    if s:
                        pool.wait_ge(act_ready, n0 + n)
                    else:
                        pool.wait_ge(act_ready, n0 + n) 
                    nc.gpsimd.tensor_tensor(prod, silu, up[:], ALU.mult).then_inc(act_mul, 1)
            def hgrn2(s):
                with pool.Fori(0, HEADS) as j:
                    pool.wait_ge(end_ready, j + 1)
                    pool.wait_ge(key_made, j + 1)
                    pool.wait_ge(k_transposed, j)
                    nc.gpsimd.tensor_tensor(k_end[:], key[:], e_end[:], ALU.mult).then_inc(k_end_ready, 1)
                    pool.wait_ge(q_silu, j + 1)
                    pool.wait_ge(o_made, j)
                    nc.gpsimd.tensor_tensor(q_int[:], q_act[:], e_all[:], ALU.mult).then_inc(q_int_ready, 1)

            def deltanet(s):
                TTp = nc.gpsimd.tensor_tensor
                pool.wait_ge(sum_ready, 2 * s)
                nc.gpsimd.memset(low_mask[:], 1.0).then_inc(masks_made, 1)
                nc.gpsimd.memset(up_mask[:], 1.0).then_inc(masks_made, 1)
                nc.gpsimd.memset(pair_mask[:], 1.0).then_inc(masks_made, 1)
                made = 3
                cuts = []
                for l in range(LEVELS):
                    m = 1 << l
                    n = P // (2 * m)
                    lo_b, up_b = low_mask[:, l, :], up_mask[:, l, :]
                    for t, rows, cols in (((lo_b,), (m, 2 * m), (0, m)), ((up_b,) + ((pair_mask[:],) if l == 0 else ()), (0, m), (m, 2 * m))):
                        for dst in t:
                            cuts.append((dst, m, n, -rows[0], 1, [[-2 * m, n], [0, 2 * m]]))
                            cuts.append((dst, m, n, rows[1] - 1, -1, [[2 * m, n], [0, 2 * m]]))
                            if cols[0] == 0:
                                cuts.append((dst, m, n, m - 1, 0, [[0, n], [-1, 2 * m]]))
                            else:
                                cuts.append((dst, m, n, -m, 0, [[0, n], [1, 2 * m]]))
                for dst, m, n, base, cm, pattern in cuts:
                    pool.wait_ge(masks_made, made)
                    view = dst.rearrange("p (n r) -> p n r", r=2 * m)
                    nc.gpsimd.affine_select(out=view, in_=view, compare_op=ALU.is_ge, fill=0.0, base=base, pattern=pattern,
                                            channel_multiplier=cm).then_inc(masks_made, 1)
                    made += 1
                assert made == N_MASKS
                with pool.Fori(0, GROUPS) as g:
                    pool.wait_ge(eg_ready, g + 1)
                    pool.wait_ge(qn_ready, g + 1)
                    pool.wait_ge(og_made, 2 * g)
                    for e in range(2):
                        TTp(q_g[:, e, :], qn, g_bc[:, e, :], ALU.mult).then_inc(qg_ready, 1)
                    for e in range(2):
                        pool.wait_ge(pt_ready, 2 * g + e + 1)
                        TTp(attn[:, e, :, :], attn[:, e, :, :], upper[:].unsqueeze(1).to_broadcast([P, NT, P]), ALU.mult).then_inc(pt_masked, 1)

            nc.gpsimd.memset(ident[:], 0.0).then_inc(ident_made, 1)
            nc.gpsimd.memset(upper[:], 1.0).then_inc(ident_made, 1)
            pool.wait_ge(ident_made, 2)
            nc.gpsimd.affine_select(out=ident[:], in_=ident[:], compare_op=ALU.not_equal, fill=1.0, base=0,
                                    pattern=[[-1, P]], channel_multiplier=1).then_inc(ident_made, 1)
            nc.gpsimd.affine_select(out=upper[:], in_=upper[:], compare_op=ALU.is_ge, fill=0.0, base=0,
                                    pattern=[[1, P]], channel_multiplier=-1).then_inc(ident_made, 1)
            for s, kind in enumerate(kinds):
                sum8(2 * s)
                {"ffn": ffn, "hg": hgrn2, "gd": deltanet}[kind](s)
                sum8(2 * s + 1)

        @block.tensor
        def _(pe):
            PASSES = ((0, 0), (0, 1), (1, 0))

            def sum_partitions(q):
                pe.wait_ge(acc_done, KD * (q + 1))
                wait(pe, rms_logged, q)
                nc.tensor.matmul(bank[4][:], ones[:], acc[:], start=True, stop=True).then_inc(sum_ready, 1)

            def blocks(dst, u, cols, moving, ks, first, last):
                r = u[0] % RING
                for n, k in enumerate(ks):
                    for wl, ml in PASSES:
                        w = (w_hi, w_lo)[wl][:, r, (cols + n) * P:(cols + n + 1) * P]
                        ins = nc.tensor.matmul(dst, w, moving[ml][:, k, :],
                                               start=first and n == 0 and (wl, ml) == (0, 0),
                                               stop=last and n == len(ks) - 1 and wl == 1)
                return ins

            def head_start(s):
                u0 = first_unit[s]
                pe.wait_ge(lo_split, u0 + RING)
                for k in range(KD):
                    pe.wait_ge(h_ready, KD * s + k + 1)
                    for q in range(RING):
                        ins = blocks(bank[q][:], (u0 + q, 0), k, (h_hi, h_lo), [k], k == 0, k == KD - 1)
                        if k == KD - 1:
                            ins.then_inc(unit_used, 1)
                sum_partitions(2 * s)

            def ffn(s):
                u0 = first_unit[s]
                n0 = ffn_no[s] * KF
                head_start(s)
                with pe.Fori(1, 2 * KF // RING) as i:
                    for q in range(RING):
                        u = (u0 + q, 4 * i)
                        pe.wait_ge(lo_split, count(u) + 1)
                        if q % 2 == 0:
                            pe.wait_ge(gate_scaled, n0 + 2 * i + q // 2 - 1)
                        else:
                            pe.wait_ge(up_scaled, n0 + 2 * i + q // 2 - 1)
                        blocks(bank[q][:], u, 0, (h_hi, h_lo), range(KD), True, True).then_inc(unit_used, 1)
                def ready(k):
                    if k in (0, KF - 2, KF - 1):
                        pe.wait_ge(act_ready, n0 + max(k + 1, KF - 2))
                out_proj(s, (act_hi, act_lo), ready)

            def out_proj(s, moving, ready):
                cuts = CUTS[kinds[s]]
                n_u = len(cuts) - 1
                tiles = RING // n_u
                v0 = first_unit[s] + IN_UNITS[kinds[s]]

                def four(i, peeled=False):
                    for t in range(max(tiles, 2)):
                        c = tiles * i + t
                        if not peeled or t >= 2:
                            pe.wait_ge(sq_done, KD * (2 * s + 1) + c - 1)
                        for q in range(n_u):
                            k = t * n_u + q
                            u = (v0 + k, 4 * i) if not isinstance(i, int) else (v0 + k + 4 * i, 0)
                            pe.wait_ge(lo_split, count(u) + 1)
                            if peeled and t == 0:
                                for k in range(cuts[q], cuts[q + 1]):
                                    ready(k)
                                    ins = blocks(bank[t % 2][:], u, k - cuts[q], moving, [k], k == 0, k == cuts[-1] - 1)
                            else:
                                ins = blocks(bank[t % 2][:], u, 0, moving, range(cuts[q], cuts[q + 1]), q == 0, q == n_u - 1)
                            ins.then_inc(unit_used, 1)
                step = max(tiles, 2) // tiles
                four(0, True)
                with pe.Fori(step, KD // tiles, step) as i:
                    four(i)
                sum_partitions(2 * s + 1)

            def hgrn2(s):
                u0 = first_unit[s]
                MM = nc.tensor.matmul
                head_start(s)

                def step(j, gemm, chain):
                    free = (q_scaled, g_scaled, f_scaled, i_scaled)

                    def piece(t, p):
                        if not gemm:
                            return
                        u = (u0 + t, 4 * j)
                        if p == 0:
                            pe.wait_ge(lo_split, count(u) + 1)
                            pe.wait_ge(free[t], j + (t >= 2))
                        ins = blocks(bank[t % 2][:], u, 2 * p, (h_hi, h_lo), [2 * p, 2 * p + 1], p == 0, p == 3)
                        if p == 3:
                            ins.then_inc(unit_used, 1)

                    piece(0, 0)
                    if chain:
                        pe.wait_ge(ident_made, 4)
                        pe.wait_ge(i_scaled, j)
                        pe.wait_ge(q_scaled, j)
                        wait(pe, o_normed, j - 1)
                        for t in range(NT):
                            ins = nc.tensor.transpose(bank[2][:, t * P:(t + 1) * P], v_fm[:, t * P:(t + 1) * P], ident[:])
                        ins.then_inc(v_transposed, 1)
                        pe.wait_ge(k_end_ready, j)
                        pe.wait_ge(g_scaled, j)
                        wait(pe, o_logged, j - 1)
                        for t in range(NT):
                            ins = nc.tensor.transpose(bank[3][:, t * P:(t + 1) * P], k_end[:, t * P:(t + 1) * P], ident[:])
                        ins.then_inc(k_transposed, 1)
                    piece(0, 1)
                    if chain:
                        pe.wait_ge(k_cen_ready, j)
                        pe.wait_ge(q_cen_ready, j)
                        wait(pe, probs_ready, j - 1)
                        for t in range(NT):
                            ins = MM(bank[5][:, t * P:(t + 1) * P], k_cen[:, t * P:(t + 1) * P],
                                     q_cen[:, t * P:(t + 1) * P], start=True, stop=True)
                        ins.then_inc(scores_made, 1)
                    piece(0, 2)
                    piece(0, 3)
                    if chain:
                        pe.wait_ge(v_copied, j)
                        pe.wait_ge(k_copied, j)
                        wait(pe, state_ready, (NCH - 1) * (j - 1))
                        for n in range(NCH - 1):
                            r0 = n % 2 * CH
                            ins = MM(bank[6 + n % 2][:, n // 2 * P:(n // 2 + 1) * P], k_tok[r0:r0 + CH, n // 2, :],
                                     v_tok[r0:r0 + CH, n // 2, :], start=True, stop=True)
                        ins.then_inc(ds_made, 1)
                    for p in range(4):
                        piece(1, p)
                    if chain:
                        pe.wait_ge(probs_ready, j)
                        pe.wait_ge(q_int_ready, j)
                        pe.wait_ge(state_ready, (NCH - 1) * j)
                        for t in range(NT):
                            MM(bank[2][:, t * P:(t + 1) * P], v_tok[:, t, :], probs[:, t, :], start=True, stop=False)
                            for n in (2 * t, 2 * t + 1):
                                if n:
                                    ins = MM(bank[2][:, n * CH:(n + 1) * CH], state[:, n - 1, :],
                                             q_int[:, n * CH:(n + 1) * CH], start=False, stop=n % 2 == 1)
                        ins.then_inc(o_made, 1)
                    for p in range(3):
                        piece(2, p)
                    if chain:
                        pe.wait_ge(o_squared, j)
                        MM(bank[3][:], ones[:], osq[:], start=True, stop=True).then_inc(o_summed, 1)
                    piece(2, 3)
                    for p in range(4):
                        piece(3, p)
                with pe.Fori(1, HEADS) as j:
                    step(j, True, True)
                step(HEADS, False, True)

                def ready(k):
                    pe.wait_ge(o_ready, k + 1)
                out_proj(s, (o_hi, o_lo), ready)

            def deltanet(s):
                MM = nc.tensor.matmul
                head_start(s)
                u0 = first_unit[s]

                def tile(u, b, need):
                    pe.wait_ge(lo_split, count(u) + 1)
                    pe.wait_ge(drained, need)
                    blocks(bank[b][:], u, 0, (h_hi, h_lo), range(KD), True, True).then_inc(unit_used, 1)
                tile((u0 + 4, 0), 0, 1)
                pe.wait_ge(ab_dve, 5)
                pe.wait_ge(ab_act, 1)
                for t in range(NT):
                    ins = nc.tensor.transpose(bank[6][:, t * AB:(t + 1) * AB], g_row_tile[:, t * P:(t + 1) * P], ident[0:AB, 0:AB])
                ins.then_inc(ab_trans, 1)
                pe.wait_ge(ab_dve, 6)
                MM(bank[7][:, 0:NT * VH], ident[:, P - 1:P].to_broadcast([P, P]), tab[:, 0, :, :].rearrange("p t h -> p (t h)"), start=True, stop=True).then_inc(last_made, 1)
                tile((u0 + 5, 0), 1, 2)
                tile((u0 + 6, 0), 0, 5)

                def step(j, d, pair, gemm, chain):
                    g = j - 1
                    at = [0]

                    def piece(n=1):
                        if not gemm:
                            return
                        for _ in range(n):
                            i, p = at[0] // 6, at[0] % 6
                            at[0] += 1
                            u = gd_unit(s, i, d, pair)
                            if p == 0:
                                pe.wait_ge(lo_split, count(u) + 1)
                                pe.wait_ge(drained, 6 * j + 1 + i - (i > 0))
                            r = u[0] % RING
                            for x in range(4 * p, 4 * p + 4):
                                k, (wl, ml) = x // 3, PASSES[x % 3]
                                ins = MM(bank[i % 2][:], (w_hi, w_lo)[wl][:, r, k * P:(k + 1) * P], (h_hi, h_lo)[ml][:, k, :],
                                         start=x == 0, stop=x == 23)
                            if p == 5:
                                ins.then_inc(unit_used, 1)

                    def tiles(b, lhs, rhs, sem_):
                        for t in range(NT):
                            ins = MM(bank[b][:, t * P:(t + 1) * P], lhs(t), rhs(t), start=True, stop=True)
                        ins.then_inc(sem_, 1)

                    if chain:
                        for e in range(2):
                            pe.wait_ge(qk_squared, 2 * g + e + 1)
                            wait(pe, og_normed, 2 * g)
                            MM(bank[2 + e][:], ones[:], y[:, e, :], start=True, stop=True).then_inc(qk_summed, 1)
                    piece()
                    if chain:
                        for e in range(2):
                            pe.wait_ge(qkv_silu, 4 * (g + 1))
                            for t in range(NT):
                                ins = nc.tensor.transpose(bank[4 + e][:, t * P:(t + 1) * P], v_a[:, e, t * P:(t + 1) * P], ident[:])
                            ins.then_inc(v_trans, 1)
                    piece(2)
                    if chain:
                        pe.wait_ge(kn_ready, g + 1)
                        wait(pe, on_logged, 2 * g)
                        tiles(7, lambda t: kn[:, t * P:(t + 1) * P], lambda t: kn[:, t * P:(t + 1) * P], kk_made)
                        for t in range(NT):
                            ins = nc.tensor.transpose(bank[6][:, t * P:(t + 1) * P], kn[:, t * P:(t + 1) * P], ident[:])
                        ins.then_inc(k_trans, 1)
                        pe.wait_ge(qn_ready, g + 1)
                        tiles(2, lambda t: kn[:, t * P:(t + 1) * P], lambda t: qn[:, t * P:(t + 1) * P], qk_made)
                    piece(5)
                    if chain:
                        for e in range(2):
                            pe.wait_ge(x_init, 2 * g + e + 1)
                            pe.wait_ge(vt_ready, 2 * g + e + 1)
                            for t in range(NT):
                                ins = nc.tensor.transpose(bank[3 + e][:, t * P:(t + 1) * P], inv_t[:, e, t, :], ident[:])
                            ins.then_inc(x_trans, 1)
                    for l in range(1, LEVELS):
                        piece()
                        last = l == LEVELS - 1
                        if chain:
                            for e in range(2):
                                pe.wait_ge(t_ready, 2 * g + e + 1)
                                pe.wait_ge(kt_ready, g + 1)
                                pe.wait_ge(vt_ready, 2 * g + 2)
                                wait(pe, t_upd, 10 * g + 2 * (l - 1) - (1 - e) if l > 1 else 0)
                                tiles(5 + e, lambda t: neg_at[:, e, t, :], lambda t: inv[:, e, t, :], p_made)
                        piece()
                        if chain:
                            for e in range(2):
                                pe.wait_ge(p_ready, 12 * g + 2 * (l - 1) + e + 1)
                                pe.wait_ge(pt_ready, 2 * g + 2)
                                if l > 1:
                                    pe.wait_ge(x_upd, 12 * g + 2 * (l - 1))
                                    pe.wait_ge(t_upd, 10 * g + 2 * (l - 1))
                                if not last:
                                    tiles((7, 2)[e], lambda t: inv_t[:, e, t, :], lambda t: prod_at[:, e, t, :], tt_made)
                                tiles(3 + e, lambda t: prod_at[:, e, t, :], lambda t: inv_t[:, e, t, :], xx_made)
                    for t in range(NT):
                        if t:
                            if chain:
                                for e in range(2):
                                    pe.wait_ge(mem_ready, 6 * g + 2 * (t - 1) + e + 1)
                                    MM(bank[3 + e][:, 0:P], kn[:, t * P:(t + 1) * P], mem[:, e, t % 2, :], start=True, stop=True).then_inc(ks_made, 1)
                        piece()
                        if chain:
                            for e in range(2):
                                if t:
                                    pe.wait_ge(r_made, 6 * g + 2 * (t - 1) + e + 1)
                                else:
                                    pe.wait_ge(x_upd, 12 * (g + 1))
                                rhs = resid_v[:, e, :] if t else vt[:, e, 0, :]
                                MM(bank[5 + e][:, 0:P], inv_t[:, e, t, :], rhs, start=True, stop=True).then_inc(wr_made, 1)
                            if t:
                                pe.wait_ge(qg_ready, 2 * (g + 1))
                                for e in range(2):
                                    MM(bank[(7, 2)[e]][:, t * P:(t + 1) * P], mem[:, e, t % 2, :], q_g[:, e, t * P:(t + 1) * P], start=True, stop=False)
                        piece()
                        if chain:
                            for e in range(2):
                                pe.wait_ge(vn_ready, 8 * g + 2 * t + e + 1)
                                pe.wait_ge(pt_masked, 2 * g + e + 1)
                                ins = MM(bank[(7, 2)[e]][:, t * P:(t + 1) * P], v_new[:, e, :], attn[:, e, t, :], start=t == 0, stop=True)
                                if t == NT - 1:
                                    ins.then_inc(og_made, 1)
                                else:
                                    pe.wait_ge(vd_ready, 8 * g + 2 * t + e + 1)
                                    MM(bank[3 + e][:, 0:P], kt[:, t * P:(t + 1) * P], v_dec[:, e, :], start=True, stop=True).then_inc(s_made, 1)
                        if t < NT - 1:
                            piece()
                    piece()
                    if chain:
                        for e in range(2):
                            pe.wait_ge(og_squared, 2 * g + e + 1)
                            MM(bank[5 + e][:], ones[:], y[:, e, :], start=True, stop=True).then_inc(on_summed, 1)
                    if gemm:
                        piece(36 - at[0])
                with pe.Fori(0, 3) as k:
                    step(2 * k + 1, 1, k, True, True)
                    step(2 * k + 2, 2, k, True, True)
                step(7, 1, 3, True, True)
                step(8, 2, 3, False, True)

                class Halves:
                    def __init__(self, a, b):
                        self.a, self.b = a, b

                    def __getitem__(self, at):
                        k = at[1]
                        return self.a[:, k, :] if k < KD else self.b[:, k - KD, :]

                def ready(k):
                    pe.wait_ge(go_ready, k + 1)
                out_proj(s, (Halves(h_hi, go_hi_b), Halves(go_lo_a, go_lo_b)), ready)

            for s, kind in enumerate(kinds):
                {"ffn": ffn, "hg": hgrn2, "gd": deltanet}[kind](s)


def pack_cols(np, w):
    k, n = w.shape
    return np.ascontiguousarray(w.reshape(k // P, P, n // P, P).transpose(2, 1, 0, 3)).reshape(n // P, P, k)



def kernel(**inputs):
    import numpy as np
    import concourse.bacc as bacc
    from concourse.bass_utils import run_bass_kernel_spmd

    a = {k: np.asarray(v) for k, v in inputs.items()}

    def in_ffn(w):
        return pack_cols(np, w).reshape(2, KF, P, UNIT).transpose(1, 0, 2, 3).reshape(2 * KF, P, UNIT)

    ffn_ins = (a["ffn1_w_in"][0], a["ffn2_w_in"][0], a["ffn1_w_in"][1], a["ffn2_w_in"][1])
    ffn_outs = (a["ffn1_w_out"][0], a["ffn2_w_out"][0], a["ffn1_w_out"][1], a["ffn2_w_out"][1])
    hg = pack_cols(np, a["hg_w_in"][0]).reshape(4, HEADS, P, UNIT)[[1, 2, 0, 3]].transpose(1, 0, 2, 3)
    gd = a["gd_w_in"][0]
    wide = 6 * GROUPS * P
    ab_w = np.zeros((D, P), gd.dtype)
    ab_w[:, 0:VH] = gd[:, wide:wide + VH]
    ab_w[:, AB - VH:AB] = gd[:, wide + VH:]
    order = [t for j in range(GROUPS) for t in (j, GROUPS + j, 2 * GROUPS + 2 * j, 2 * GROUPS + 2 * j + 1,
                                                4 * GROUPS + 2 * j, 4 * GROUPS + 2 * j + 1)]
    gd_tiles = pack_cols(np, np.ascontiguousarray(gd[:, :wide]))[order]
    conv_order = [t for t in order if t < 4 * GROUPS]
    ab_params = np.zeros((AB, 2), a["gd_dt_bias"].dtype)
    ab_params[AB - VH:, 0] = a["gd_dt_bias"][0]
    ab_params[AB - VH:, 1] = a["gd_a_log"][0]
    arrays = {
        "x": a["x"][0].T.reshape(KD, P, TOK).transpose(1, 0, 2),
        "gains": a["norm_gains"].reshape(12, KD, P).transpose(2, 0, 1).reshape(P, 12 * KD),
        "ffn_in": np.concatenate([in_ffn(w) for w in ffn_ins]),
        "ffn_out": np.concatenate([pack_cols(np, w) for w in ffn_outs]),
        "hg_in": hg.reshape(4 * HEADS, P, UNIT),
        "hg_out": pack_cols(np, a["hg_w_out"][0]),
        "hg_bounds": a["hg_lower_bounds"][0].reshape(HEADS, P).T,
        "hg_gain": a["hg_norm_gain"][0].reshape(P, 1),
        "gd_in": np.concatenate([pack_cols(np, ab_w), gd_tiles]),
        "gd_out": pack_cols(np, a["gd_w_out"][0]),
        "gd_conv": a["gd_conv_w"][0].reshape(TAPS, 4 * GROUPS, P)[:, conv_order].transpose(2, 1, 0).reshape(P, GROUPS, 4, TAPS),
        "gd_ab": ab_params,
        "gd_gain": a["gd_norm_gain"][0].reshape(P, 1),
    }
    arrays = {"in_" + k: np.ascontiguousarray(v) for k, v in arrays.items()}
    nc = bacc.Bacc("TRN2", target_bir_lowering=False, num_devices=1)
    A = {k[3:]: nc.dram_tensor(k, v.shape, mybir.dt.float32, kind="ExternalInput").ap() for k, v in arrays.items()}
    out = nc.dram_tensor("out", (P, KD, TOK), mybir.dt.float32, kind="ExternalOutput").ap()
    trunk(nc, A, out)
    got = run_bass_kernel_spmd(nc, [arrays], core_ids=[0]).results[0]["out"]
    return np.ascontiguousarray(got.transpose(1, 0, 2).reshape(D, TOK).T).reshape(1, TOK, D)
```

```python
import concourse.bass as bass
from concourse import mybir
from contextlib import ExitStack

P = 128
TOK = 512
D = 1024
KD = D // P
FF = 2816
KF = FF // P
UNIT = KD * P
RING = 4
HEADS = 8
CH = 64
NCH = TOK // CH
NT = TOK // P
GROUPS = 8
VH = 16
TAPS = 4
LEVELS = 7
AB = 48
CUTS = {"ffn": [0, 6, 12, 17, 22], "hg": [0, 8], "gd": [0, 8, 16]}


def trunk(nc, A, out, kinds=("ffn", "hg", "ffn", "ffn", "gd", "ffn")):
    f32 = mybir.dt.float32
    f32r = mybir.dt.float32r
    i8 = mybir.dt.int8
    ALU = mybir.AluOpType
    ACT = mybir.ActivationFunctionType
    IN_UNITS = {"ffn": 2 * KF, "hg": 4 * HEADS, "gd": 1 + 6 * GROUPS}
    N_UNITS = {k: n + KD * (len(CUTS[k]) - 1) for k, n in IN_UNITS.items()}
    first_unit, total = [], 0
    for kind in kinds:
        first_unit.append(total)
        total += N_UNITS[kind]
    ffn_no = {s: n for n, s in enumerate(s for s, k in enumerate(kinds) if k == "ffn")}
    LAST = len(kinds)

    ctx = ExitStack()
    with ctx:
        def sb(name, shape, dt=f32):
            return ctx.enter_context(nc.sbuf_tensor(name, shape, dt))

        def sem(name):
            return ctx.enter_context(nc.semaphore(name))

        x = sb("resid", [P, KD, TOK])
        h_hi = sb("h_hi", [P, KD, TOK], f32r)
        with nc.sbuf_tensor("m", [P, KD, TOK], f32) as m:
            pass
        h_lo = sb("h_lo", [P, KD, TOK], f32r)
        raw = sb("raw", [P, RING, UNIT])
        w_hi = sb("w_hi", [P, RING, UNIT], f32r)
        w_lo = sb("w_lo", [P, RING, UNIT], f32r)
        gains = sb("gain_table", [P, 12 * KD])
        half_gains = sb("half_gains", [P, 12 * KD])
        ones = sb("ones", [P, P])
        eps = sb("eps", [P, 1])
        sq = sb("sq", [P, 2, TOK])
        acc = sb("acc", [P, TOK])
        rms = sb("rms", [P, 2, TOK])
        y = sb("y", [P, 2, TOK])
        gate = sb("gate", [P, TOK])
        up = sb("up", [P, TOK])
        ident = sb("ident", [P, P])
        upper = sb("upper", [P, P])
        with ExitStack() as region:
            def part(name, shape, dt=f32):
                return region.enter_context(nc.sbuf_tensor(name, shape, dt))
            act_hi = part("act_hi", [P, KF, TOK], f32r)
            act_lo = part("act_lo", [P, KF, TOK], f32r)
        with ExitStack() as region:
            def part(name, shape, dt=f32):
                return region.enter_context(nc.sbuf_tensor(name, shape, dt))
            o_hi = part("o_hi", [P, HEADS, TOK], f32r)
            o_lo = part("o_lo", [P, HEADS, TOK], f32r)
            f_in, g_in = gate, up
            (sig, forget, key, logf, b, b_mid, b_end, e_pos, e_neg, e_all, e_end, v_fm, q_in, q_act, g_act,
             q_cen, k_cen, q_int, k_end, osq, o_rms, o_fm) = [part(n, [P, TOK]) for n in (
                "sig", "forget", "key", "logf", "b", "b_mid", "b_end", "e_pos", "e_neg", "e_all", "e_end", "v_fm",
                "q_in", "q_act", "g_act", "q_cen", "k_cen", "q_int", "k_end", "osq", "o_rms", "o_fm")]
            v_tok = part("v_tok", [P, NT, P])
            k_tok = part("k_tok", [P, NT, P])
            probs = part("probs", [P, NT, P])
            state = part("state", [P, NCH - 1, P])
            scan_keep = part("scan_keep", [P, TOK])
            causal = part("causal", [P, P])
            bound = part("bound", [P, HEADS])
            bound_rest = part("bound_rest", [P, HEADS])
            bound_tmp = part("bound_tmp", [P, 3, HEADS])
            hg_gain = part("hg_gain", [P, 1])
        with ExitStack() as region:
            def part(name, shape, dt=f32):
                return region.enter_context(nc.sbuf_tensor(name, shape, dt))
            gd_o = part("gd_o", [P, VH, TOK])
            with ExitStack() as inner:
                def late(name, shape, dt=f32):
                    return inner.enter_context(nc.sbuf_tensor(name, shape, dt))
                go_lo_a = late("go_lo_a", [P, KD, TOK], f32r)
                go_hi_b = late("go_hi_b", [P, KD, TOK], f32r)
                go_lo_b = late("go_lo_b", [P, KD, TOK], f32r)
            pre = part("pre", [P, TAPS - 1 + TOK])
            q_a = part("q_a", [P, TOK])
            k_a = part("k_a", [P, TOK])
            v_a = part("v_a", [P, 2, TOK])
            z_a = part("z_a", [P, 2, TOK])
            vt = part("vt", [P, 2, NT, P])
            g_bc = part("g_bc", [P, 2, TOK])
            q_g = part("q_g", [P, 2, TOK])
            attn = part("attn", [P, 2, NT, P])
            neg_at = part("neg_at", [P, 2, NT, P])
            inv = part("inv", [P, 2, NT, P])
            inv_t = part("inv_t", [P, 2, NT, P])
            prod_at = part("prod_at", [P, 2, NT, P])
            resid_v = part("resid_v", [P, 2, P])
            v_new = part("v_new", [P, 2, P])
            v_dec = part("v_dec", [P, 2, P])
            mem = part("mem", [P, 2, 2, P])
            low_mask = part("low_mask", [P, LEVELS, P], i8)
            up_mask = part("up_mask", [P, LEVELS, P], i8)
            pair_mask = part("pair_mask", [P, P])
            tab = part("tab", [P, 6, NT, VH])
            spare = part("spare", [P, 2])
            gtab = part("gtab", [P, 6, NT, 2])
            conv_w = part("conv_w", [P, GROUPS, 4, TAPS])
            gd_gain = part("gd_gain", [P, 1])
            gd_ab = part("gd_ab", [AB, 2])
            ea = part("ea", [AB, 1])
        qn, kn = sq[:, 0, :], sq[:, 1, :]
        ab_in = attn[:].rearrange("p e t c -> p (e t c)")[0:AB, 0:TOK]
        ab_exp = attn[:].rearrange("p e t c -> p (e t c)")[0:AB, TOK:2 * TOK]
        keep_rows = neg_at[:].rearrange("p e t c -> p (e t c)")[0:AB, 0:TOK]
        g_step = neg_at[:].rearrange("p e t c -> p (e t c)")[0:AB, TOK:2 * TOK]
        g_row_tile = inv[:].rearrange("p e t c -> p (e t c)")[0:AB, 0:TOK]
        tab_t = inv[:].rearrange("p e t c -> p (e t c)")[:, TOK:TOK + NT * AB].rearrange("p (t h) -> p t h", h=AB)
        kt = acc
        silu = y[:, 0, :]
        prod = y[:, 1, :]
        bank = [ctx.enter_context(nc.psum_tensor(f"bank{i}", [P, TOK], f32)) for i in range(8)]

        raw_loaded = [sem(f"raw_loaded{i}") for i in range(RING)]
        hi_split = sem("hi_split")
        lo_split = sem("lo_split")
        unit_used = sem("unit_used")
        first_loaded = [sem(f"first_loaded{k}") for k in range(KD)]
        const_loaded = sem("const_loaded")
        const_made = sem("const_made")
        sq_done = sem("sq_done")
        acc_done = sem("acc_done")
        sum_ready = sem("sum_ready")
        rms_logged = sem("rms_logged")
        rms_ready = sem("rms_ready")
        m_copied = sem("m_copied")
        y_scaled = sem("y_scaled")
        x_ready = sem("x_ready")
        h_hi_ready = sem("h_hi_ready")
        h_ready = sem("h_ready")
        gate_scaled = sem("gate_scaled")
        up_scaled = sem("up_scaled")
        gate_silu = sem("gate_silu")
        act_mul = sem("act_mul")
        act_hi_ready = sem("act_hi_ready")
        act_ready = sem("act_ready")
        stored = sem("stored")
        masks_made = sem("masks_made")
        ab_loaded = sem("ab_loaded")
        ab_dve = sem("ab_dve")
        ab_act = sem("ab_act")
        ab_trans = sem("ab_trans")
        last_made = sem("last_made")
        g_stored = sem("g_stored")
        g_loaded = sem("g_loaded")
        gtab_ready = sem("gtab_ready")
        drained = sem("drained")
        conv_mac = sem("conv_mac")
        qkv_silu = sem("qkv_silu")
        z_silu = sem("z_silu")
        qk_squared = sem("qk_squared")
        qk_summed = sem("qk_summed")
        qk_logged = sem("qk_logged")
        qk_root = sem("qk_root")
        qn_ready = sem("qn_ready")
        kn_ready = sem("kn_ready")
        v_trans = sem("v_trans")
        vt_ready = sem("vt_ready")
        k_trans = sem("k_trans")
        kt_ready = sem("kt_ready")
        kk_made = sem("kk_made")
        qk_made = sem("qk_made")
        d_made = sem("d_made")
        gam_ready = sem("gam_ready")
        eg_ready = sem("eg_ready")
        at_ready = sem("at_ready")
        pt_ready = sem("pt_ready")
        pt_masked = sem("pt_masked")
        qg_ready = sem("qg_ready")
        xi_mul = sem("xi_mul")
        x_init = sem("x_init")
        x_trans = sem("x_trans")
        t_ready = sem("t_ready")
        p_made = sem("p_made")
        p_ready = sem("p_ready")
        xt_made = sem("xt_made")
        x_copied = sem("x_copied")
        tt_made = sem("tt_made")
        t_upd = sem("t_upd")
        xx_made = sem("xx_made")
        x_upd = sem("x_upd")
        x_gate = sem("x_gate")
        ks_made = sem("ks_made")
        r_made = sem("r_made")
        wr_made = sem("wr_made")
        vd_ready = sem("vd_ready")
        vn_ready = sem("vn_ready")
        s_made = sem("s_made")
        mem_ready = sem("mem_ready")
        og_made = sem("og_made")
        og_squared = sem("og_squared")
        on_summed = sem("on_summed")
        on_logged = sem("on_logged")
        on_root = sem("on_root")
        og_normed = sem("og_normed")
        og_ready = sem("og_ready")
        go_hi = sem("go_hi")
        go_ready = sem("go_ready")
        ident_made = sem("ident_made")
        hg_const = sem("hg_const")
        hg_loaded = sem("hg_loaded")
        f_scaled = sem("f_scaled")
        f_sig = sem("f_sig")
        forget_made = sem("forget_made")
        key_made = sem("key_made")
        f_logged = sem("f_logged")
        b_scanned = sem("b_scanned")
        b_centered = sem("b_centered")
        b_ended = sem("b_ended")
        pos_ready = sem("pos_ready")
        neg_ready = sem("neg_ready")
        all_ready = sem("all_ready")
        end_ready = sem("end_ready")
        i_scaled = sem("i_scaled")
        v_transposed = sem("v_transposed")
        v_copied = sem("v_copied")
        k_end_ready = sem("k_end_ready")
        k_transposed = sem("k_transposed")
        k_copied = sem("k_copied")
        q_scaled = sem("q_scaled")
        q_silu = sem("q_silu")
        q_cen_ready = sem("q_cen_ready")
        k_cen_ready = sem("k_cen_ready")
        q_int_ready = sem("q_int_ready")
        g_scaled = sem("g_scaled")
        g_silu = sem("g_silu")
        scores_made = sem("scores_made")
        probs_ready = sem("probs_ready")
        ds_made = sem("ds_made")
        state_ready = sem("state_ready")
        o_made = sem("o_made")
        o_squared = sem("o_squared")
        o_summed = sem("o_summed")
        o_logged = sem("o_logged")
        o_root = sem("o_root")
        o_normed = sem("o_normed")
        o_gated = sem("o_gated")
        o_hi_ready = sem("o_hi_ready")
        o_ready = sem("o_ready")
        HG_CONST = 12
        N_CONST = 16
        N_HG = 32
        POOLED = KD - 1
        SKEW = KD - RING
        if "gd" in kinds:
            g_rows = nc.dram_tensor("g_rows", [VH, TOK], f32, kind="Internal").ap()
        N_GD = 3 * 16
        N_MASKS = 3 + 3 * (2 * LEVELS + 1)

        def gd_unit(s, i, step, pair):
            u = first_unit[s] + 1 + 6 * step + i
            return (u, 12 * pair) if not isinstance(pair, int) else (u + 12 * pair, 0)

        block = ctx.enter_context(nc.Block())

        def count(u):
            return u[0] + u[1]

        def ahead(u, n):
            return (u[0] + n, u[1])

        def wait(eng, s, v):
            if not isinstance(v, int) or v > 0:
                eng.wait_ge(s, v)

        def post_gain(s, c):
            g = half_gains if kinds[s] == "ffn" else gains
            i = ((s // 3) * 6 + 2 * (s % 3) + 1) * KD + c
            return g[:, i:i + 1]

        def pre_gain(s, c):
            i = ((s // 3) * 6 + 2 * (s % 3)) * KD + c
            return gains[:, i:i + 1]

        @block.sync
        def _(sp):
            sp.dma_start(gains[:], A["gains"]).then_inc(const_loaded, 16)
            for k in range(KD):
                cols = slice(k * P, (k + 1) * P)
                sp.dma_start(x[:, k, :], A["x"][:, k, :]).then_inc(first_loaded[k], 16)
                sp.dma_start(raw[:, :, cols], A[kinds[0] + "_in"][0:RING, :, cols].rearrange("u p n -> p u n")).then_inc(first_loaded[k], 16)
            sp.wait_ge(lo_split, KD)

            def load(u, src, n=UNIT):
                if u[0] >= RING or not isinstance(u[1], int):
                    wait(sp, lo_split, count(u) - RING + 1 + SKEW)
                sp.dma_start(raw[:, u[0] % RING, 0:n], src).then_inc(raw_loaded[u[0] % RING], 16)

            def ffn(s):
                u0 = first_unit[s]
                w_in = A["ffn_in"]
                w_out = A["ffn_out"]
                row0 = ffn_no[s] * 2 * KF

                def four(i, first=0):
                    for q in range(RING):
                        row = sp.snap(row0 + 4 * i + q) if not isinstance(i, int) else row0 + 4 * i + q
                        load((u0 + q, 4 * i) if not isinstance(i, int) else (u0 + q + 4 * i, 0),
                             w_in[bass.ds(row, 1), :, :].rearrange("a p n -> (a p) n"))
                if s:
                    four(0)
                with sp.Fori(1, 2 * KF // RING) as i:
                    four(i)
                out_loads(s, w_out, ffn_no[s] * KD)

            def out_loads(s, w_out, row0):
                cuts = CUTS[kinds[s]]
                n_u = len(cuts) - 1
                tiles = RING // n_u
                v0 = first_unit[s] + IN_UNITS[kinds[s]]
                with sp.Fori(0, KD // tiles) as i:
                    for t in range(tiles):
                        for q in range(n_u):
                            row = sp.snap(row0 + tiles * i + t)
                            a, b = cuts[q] * P, cuts[q + 1] * P
                            load((v0 + t * n_u + q, 4 * i), w_out[bass.ds(row, 1), :, a:b].rearrange("a p n -> (a p) n"), b - a)

            def hgrn2(s):
                for q in range(RING if s else 0):
                    load((first_unit[s] + q, 0), A["hg_in"][q:q + 1, :, :].rearrange("a p n -> (a p) n"))
                wait(sp, sum_ready, 2 * s)
                sp.dma_start(bound_tmp[:, 0, :], A["hg_bounds"]).then_inc(hg_loaded, 16)
                sp.dma_start(hg_gain[:], A["hg_gain"]).then_inc(hg_loaded, 16)
                with sp.Fori(1, HEADS) as j:
                    for q in range(4):
                        row = sp.snap(4 * j + q)
                        load((first_unit[s] + q, 4 * j), A["hg_in"][bass.ds(row, 1), :, :].rearrange("a p n -> (a p) n"))
                out_loads(s, A["hg_out"], 0)

            def deltanet(s):
                def group(j, step, pair, tiles=range(6)):
                    for i in tiles:
                        row = sp.snap(6 * j + 1 + i) if not isinstance(j, int) else 6 * j + 1 + i
                        load(gd_unit(s, i, step, pair), A["gd_in"][bass.ds(row, 1), :, :].rearrange("a p n -> (a p) n"))

                def rows(j):
                    if isinstance(j, int):
                        wait(sp, qg_ready, 2 * j)
                    else:
                        first = sp.snap(2 * j)
                        sp.wait_ge(qg_ready, 2 * j)
                        j = None
                    src = g_rows[bass.ds(first, 2), :] if j is None else g_rows[2 * j:2 * j + 2, :]
                    sp.dma_start(g_bc[:], src.rearrange("(o h) t -> o h t", o=1).to_broadcast([P, 2, TOK])).then_inc(g_loaded, 16)

                if s:
                    load((first_unit[s], 0), A["gd_in"][0:1, :, :].rearrange("a p n -> (a p) n"))
                    group(0, 0, 0, range(RING - 1))
                wait(sp, sum_ready, 2 * s)
                sp.dma_start(conv_w[:], A["gd_conv"]).then_inc(ab_loaded, 16)
                sp.dma_start(gd_gain[:], A["gd_gain"]).then_inc(ab_loaded, 16)
                sp.dma_start(gd_ab[:], A["gd_ab"]).then_inc(ab_loaded, 16)
                group(0, 0, 0, range(RING - 1, 6))
                sp.wait_ge(ab_dve, 5)
                sp.dma_start(g_rows, g_row_tile[32:AB, :]).then_inc(g_stored, 16)
                sp.wait_ge(g_stored, 16)
                rows(0)
                group(1, 1, 0)
                rows(1)
                with sp.Fori(0, GROUPS // 2 - 1) as k:
                    for d in (2, 3):
                        group(2 * k + d, d, k)
                        rows(2 * k + d)
                out_loads(s, A["gd_out"], 0)

            for s, kind in enumerate(kinds):
                {"ffn": ffn, "hg": hgrn2, "gd": deltanet}[kind](s)
            for c in range(KD):
                sp.wait_ge(x_ready, KD * (LAST - 1) + c + 1)
                sp.dma_start(out[:, c, :], x[:, c, :]).then_inc(stored, 16)
            sp.wait_ge(stored, 16 * KD)

        @block.scalar
        def _(act):
            def split(u):
                if u[0] >= RING or not isinstance(u[1], int):
                    wait(act, unit_used, count(u) - RING + 1)
                act.wait_ge(raw_loaded[u[0] % RING], 16 * (u[0] // RING) + 4 * u[1])
                nc.scalar.activation(w_hi[:, u[0] % RING, :], raw[:, u[0] % RING, :], ACT.Copy).then_inc(hi_split, 1)

            def square(q, c, src):
                wait(act, acc_done, POOLED * q + c - 1)
                nc.scalar.activation(sq[:, c % 2, :], src, ACT.Square).then_inc(sq_done, 1)

            def root(q):
                act.wait_ge(sum_ready, q + 1)
                nc.scalar.activation(rms[:, q % 2, :], bank[4][:], ACT.Ln, bias=eps[:], scale=1.0 / D).then_inc(rms_logged, 1)
                act.wait_ge(rms_logged, q + 1)
                nc.scalar.activation(rms[:, q % 2, :], rms[:, q % 2, :], ACT.Exp, scale=-0.5).then_inc(rms_ready, 1)

            def pre(s):
                for c in range(KD):
                    if s == 0:
                        cols = slice(c * P, (c + 1) * P)
                        act.wait_ge(first_loaded[c], 32)
                        nc.scalar.activation(w_hi[:, :, cols], raw[:, :, cols], ACT.Copy).then_inc(hi_split, 1)
                        act.wait_ge(const_loaded, N_CONST)
                        act.wait_ge(const_made, 3)
                    else:
                        act.wait_ge(x_ready, KD * (s - 1) + c + 1)
                    nc.scalar.activation(h_hi[:, c, :], x[:, c, :], ACT.Copy, scale=pre_gain(s, c)).then_inc(h_hi_ready, 1)
                    square(2 * s, c, x[:, c, :])
                if s == 0:
                    act.preload_act_table_set("natural_log_exp_and_others")
                split((first_unit[s] + RING, 0))
                root(2 * s)

            def out_tile(s, c, b):
                act.wait_ge(unit_used, c[1])
                nc.scalar.activation(m[:, c[0], :], bank[b][:], ACT.Copy)

            def ffn(s):
                u0 = first_unit[s]
                n0 = ffn_no[s] * KF

                def pair(u, n, par, first=False):
                    if first:
                        split(ahead(u, 5))
                    act.wait_ge(gate_scaled, n0 + n + 1)
                    wait(act, act_mul, n0 + n)
                    nc.scalar.activation(silu, gate[:], ACT.Silu).then_inc(gate_silu, 1)
                    if not first:
                        split(ahead(u, 4))
                        split(ahead(u, 5))
                    act.wait_ge(act_mul, n0 + n + 1)
                    nc.scalar.activation(act_hi[:, bass.ds(n, 1), :].rearrange("p a n -> p (a n)"), prod, ACT.Copy).then_inc(act_hi_ready, 1)

                pair((u0, 0), 0, 0, True)
                pair((u0 + 2, 0), 1, 1)
                with act.Fori(1, KF // 2) as i:
                    pair((u0, 4 * i), 2 * i, 0)
                    pair((u0 + 2, 4 * i), 2 * i + 1, 1)
                out_tiles(s)

            def out_tiles(s):
                n_u = len(CUTS[kinds[s]]) - 1
                tiles = RING // n_u
                v0 = first_unit[s] + IN_UNITS[kinds[s]]

                def four(i, last=False):
                    for t in range(max(tiles, 2)):
                        u = (v0 + t * n_u, 4 * i) if not isinstance(i, int) else (v0 + 4 * i + t * n_u, 0)
                        c = tiles * i + t
                        more = not last or t * n_u + RING < max(tiles, 2) * n_u
                        for q in range(n_u - 1):
                            if more:
                                split(ahead(u, 4 + q))
                        act.wait_ge(unit_used, count(u) + n_u)
                        wait(act, acc_done, POOLED * (2 * s + 1) + c - 1)
                        nc.scalar.activation(sq[:, t % 2, :], bank[t % 2][:], ACT.Square).then_inc(sq_done, 1)
                        wait(act, y_scaled, KD * s)
                        nc.scalar.activation(m[:, bass.ds(c, 1), :].rearrange("p a n -> p (a n)"), bank[t % 2][:], ACT.Copy).then_inc(m_copied, 1)
                        if more:
                            split(ahead(u, 3 + n_u))
                step = max(tiles, 2) // tiles
                n = KD // tiles
                act.preload_act_table_set("natural_log_exp_and_others")
                with act.Fori(0, n - step, step) as i:
                    four(i)
                four(n - step, s == LAST - 1)
                root(2 * s + 1)

            def hgrn2(s):
                u0 = first_unit[s]

                act.wait_ge(hg_const, 4)
                nc.scalar.activation(bound_tmp[:, 2, :], bound_tmp[:, 1, :], ACT.Exp).then_inc(hg_const, 1)

                def step(j, gemm, chain):
                    u = (u0, 4 * j) if not isinstance(j, int) else (u0 + 4 * j, 0)
                    if chain:
                        act.wait_ge(v_transposed, j)
                        nc.scalar.activation(v_tok[:].rearrange("p t v -> p (t v)"), bank[2][:], ACT.Copy).then_inc(v_copied, 1)
                    if gemm and chain:
                        split(ahead(u, 4))
                    if gemm:
                        act.wait_ge(f_scaled, j + 1)
                        nc.scalar.activation(sig[:], f_in[:], ACT.Sigmoid).then_inc(f_sig, 1)
                        act.preload_act_table_set("natural_log_exp_and_others")
                        act.wait_ge(forget_made, j + 1)
                        wait(act, b_ended, j)
                        nc.scalar.activation(logf[:], forget[:], ACT.Ln).then_inc(f_logged, 1)
                        act.wait_ge(b_centered, j + 1)
                        wait(act, q_cen_ready, j)
                        nc.scalar.activation(e_pos[:], b_mid[:], ACT.Exp).then_inc(pos_ready, 1)
                        nc.scalar.activation(e_neg[:], b_mid[:], ACT.Exp, scale=-1.0).then_inc(neg_ready, 1)
                        wait(act, state_ready, (NCH - 1) * j)
                        wait(act, q_int_ready, j)
                        nc.scalar.activation(e_all[:], b[:], ACT.Exp).then_inc(all_ready, 1)
                        act.wait_ge(b_ended, j + 1)
                        nc.scalar.activation(e_end[:], b_end[:], ACT.Exp).then_inc(end_ready, 1)
                        split(ahead(u, 5))
                    if chain:
                        act.wait_ge(o_made, j)
                        nc.scalar.activation(osq[:], bank[2][:], ACT.Square).then_inc(o_squared, 1)
                    if gemm:
                        split(ahead(u, 6))
                    if chain:
                        act.wait_ge(o_summed, j)
                        wait(act, o_normed, j - 1)
                        nc.scalar.activation(o_rms[:], bank[3][:], ACT.Ln, bias=eps[:], scale=1.0 / P).then_inc(o_logged, 1)
                        act.wait_ge(o_logged, j)
                        nc.scalar.activation(o_rms[:], o_rms[:], ACT.Exp, scale=-0.5).then_inc(o_root, 1)
                        act.wait_ge(o_gated, j)
                        nc.scalar.activation(o_hi[:, bass.ds(j - 1, 1), :].rearrange("p a n -> p (a n)"), o_fm[:], ACT.Copy).then_inc(o_hi_ready, 1)
                    if gemm:
                        act.wait_ge(q_scaled, j + 1)
                        nc.scalar.activation(q_act[:], q_in[:], ACT.Silu).then_inc(q_silu, 1)
                        split(ahead(u, 7))
                        act.wait_ge(g_scaled, j + 1)
                        nc.scalar.activation(g_act[:], g_in[:], ACT.Silu).then_inc(g_silu, 1)
                step(0, True, False)
                step(1, True, True)
                with act.Fori(2, HEADS) as j:
                    step(j, True, True)
                step(HEADS, False, True)
                out_tiles(s)

            def deltanet(s):
                def copy(dst, src):
                    return nc.scalar.activation(dst, src, ACT.Copy)

                def conv_silu(j, i):
                    act.wait_ge(conv_mac, 4 * (4 * j + i + 1))
                    if i == 0:
                        wait(act, qn_ready, j)
                    elif i == 1:
                        wait(act, kn_ready, j)
                    else:
                        wait(act, v_trans, 2 * (j - 1) + i - 1)
                    dst = (q_a[:], k_a[:], v_a[:, 0, :], v_a[:, 1, :])[i]
                    nc.scalar.activation(dst, (gate, up)[i % 2][:], ACT.Silu).then_inc(qkv_silu, 1)

                def squares(g):
                    wait(act, og_ready, 2 * g)
                    act.wait_ge(qkv_silu, 4 * g + 2)
                    nc.scalar.activation(y[:, 0, :], q_a[:], ACT.Square).then_inc(qk_squared, 1)
                    nc.scalar.activation(y[:, 1, :], k_a[:], ACT.Square).then_inc(qk_squared, 1)

                def z_out(j, e):
                    act.wait_ge(drained, 6 * (j + 1) + e)
                    wait(act, og_ready, 2 * (j - 1) + e + 1)
                    nc.scalar.activation(z_a[:, e, :], (gate, up)[e][:], ACT.Silu).then_inc(z_silu, 1)

                def betas():
                    act.wait_ge(ab_dve, 1)
                    act.wait_ge(drained, 1)
                    nc.scalar.activation(g_row_tile[0:VH, :], ab_in[0:VH, :], ACT.Sigmoid).then_inc(ab_act, 1)
                    act.preload_act_table_set("natural_log_exp_and_others")
                    act.wait_ge(ab_dve, 2)
                    nc.scalar.activation(ab_exp[32:AB, :], ab_in[32:AB, :], ACT.Abs).then_inc(ab_act, 1)
                    act.wait_ge(ab_act, 2)
                    nc.scalar.activation(ab_exp[32:AB, :], ab_exp[32:AB, :], ACT.Exp, scale=-1.0).then_inc(ab_act, 1)
                    act.wait_ge(ab_act, 3)
                    nc.scalar.activation(ab_exp[32:AB, :], ab_exp[32:AB, :], ACT.Ln, bias=ones[32:AB, 0:1]).then_inc(ab_act, 1)
                    nc.scalar.activation(ea[32:AB, :], gd_ab[32:AB, 1:2], ACT.Exp).then_inc(ab_act, 1)
                    act.wait_ge(ab_dve, 6)
                    nc.scalar.activation(tab[:, 1, :, :], tab[:, 0, :, :], ACT.Exp).then_inc(ab_act, 1)
                    act.wait_ge(last_made, 1)
                    nc.scalar.activation(tab[:, 4, :, :], bank[7][:, 0:NT * VH].rearrange("p (t h) -> p t h", h=VH), ACT.Exp).then_inc(ab_act, 1)
                    act.wait_ge(ab_dve, 9)
                    nc.scalar.activation(tab[:, 3, :, :], tab[:, 3, :, :], ACT.Exp).then_inc(ab_act, 1)

                def step(j, d, pair, gemm, chain):
                    g = j - 1

                    def done(i):
                        if gemm:
                            split(ahead(gd_unit(s, i, d, pair), 4))

                    if chain:
                        act.preload_act_table_set("natural_log_exp_and_others")
                        for e in range(2):
                            act.wait_ge(qk_summed, 2 * g + e + 1)
                            nc.scalar.activation(y[:, e, :], bank[2 + e][:], ACT.Ln, bias=eps[:]).then_inc(qk_logged, 1)
                            act.wait_ge(qk_logged, 2 * g + e + 1)
                            nc.scalar.activation(y[:, e, :], y[:, e, :], ACT.Exp, scale=-0.5).then_inc(qk_root, 1)
                        for e in range(2):
                            act.wait_ge(d_made, 2 * g + e + 1)
                            nc.scalar.activation(attn[:, e, :, :], attn[:, e, :, :], ACT.Exp).then_inc(gam_ready, 1)
                        nc.scalar.activation(g_bc[:], g_bc[:], ACT.Exp).then_inc(eg_ready, 1)
                        for e in range(2):
                            act.wait_ge(v_trans, 2 * g + e + 1)
                            copy(vt[:, e, :, :], bank[4 + e][:].rearrange("p (t v) -> p t v", v=P)).then_inc(vt_ready, 1)
                        act.wait_ge(k_trans, g + 1)
                        copy(kt[:], bank[6][:]).then_inc(kt_ready, 1)
                    if gemm:
                        done(0)
                    if chain:
                        for e in range(2):
                            act.wait_ge(x_trans, 2 * g + e + 1)
                            wait(act, p_made, 12 * g)
                            copy(inv[:, e, :, :], bank[3 + e][:].rearrange("p (t v) -> p t v", v=P)).then_inc(t_ready, 1)
                    for l in range(1, LEVELS):
                        if chain:
                            for e in range(2):
                                act.wait_ge(p_made, 12 * g + 2 * (l - 1) + e + 1)
                                copy(prod_at[:, e, :, :], bank[5 + e][:].rearrange("p (t v) -> p t v", v=P)).then_inc(p_ready, 1)
                                if l > 1:
                                    act.wait_ge(xt_made, 10 * g + 2 * (l - 2) + e + 1)
                                    copy(inv_t[:, e, :, :], bank[3 + e][:].rearrange("p (t v) -> p t v", v=P)).then_inc(x_copied, 1)
                        if gemm and l == 1:
                            conv_silu(j, 0)
                        if gemm and l == 2:
                            done(1)
                        if gemm and l == 3:
                            conv_silu(j, 1)
                        if gemm and l == 5:
                            done(2)
                        if gemm and l == 6:
                            conv_silu(j, 2)
                    if gemm:
                        done(3)
                    if chain:
                        for e in range(2):
                            act.wait_ge(og_made, 2 * g + e + 1)
                            nc.scalar.activation(y[:, e, :], bank[(7, 2)[e]][:], ACT.Square).then_inc(og_squared, 1)
                    if gemm:
                        conv_silu(j, 3)
                        done(4)
                    if chain:
                        act.preload_act_table_set("natural_log_exp_and_others")
                        for e in range(2):
                            act.wait_ge(on_summed, 2 * g + e + 1)
                            nc.scalar.activation(y[:, e, :], bank[5 + e][:], ACT.Ln, bias=eps[:], scale=1.0 / P).then_inc(on_logged, 1)
                            act.wait_ge(on_logged, 2 * g + e + 1)
                            nc.scalar.activation(y[:, e, :], y[:, e, :], ACT.Exp, scale=-0.5).then_inc(on_root, 1)
                    if gemm:
                        z_out(j, 0)
                        done(5)
                        squares(j)
                        z_out(j, 1)

                act.wait_ge(ab_loaded, N_GD)
                split(ahead((first_unit[s] + 1, 0), 4))
                betas()
                for i in range(4):
                    conv_silu(0, i)
                    if 0 < i < 3:
                        split(ahead((first_unit[s] + 1 + i, 0), 4))
                for i in (3, 4):
                    split(ahead((first_unit[s] + 1 + i, 0), 4))
                z_out(0, 0)
                split(ahead((first_unit[s] + 6, 0), 4))
                z_out(0, 1)
                squares(0)
                step(1, 1, 0, True, True)
                with act.Fori(0, GROUPS // 2 - 1) as k:
                    step(2 * k + 2, 2, k, True, True)
                    step(2 * k + 3, 3, k, True, True)
                step(GROUPS, 0, 0, False, True)
                for k in range(VH):
                    act.wait_ge(og_ready, k + 1)
                    dst = h_hi[:, k, :] if k < KD else go_hi_b[:, k - KD, :]
                    copy(dst, gd_o[:, k, :]).then_inc(go_hi, 1)
                out_tiles(s)

            for s, kind in enumerate(kinds):
                pre(s)
                {"ffn": ffn, "hg": hgrn2, "gd": deltanet}[kind](s)

        @block.vector
        def _(dve):
            def split(u):
                dve.wait_ge(hi_split, count(u) + 1 + SKEW)
                r = u[0] % RING
                nc.vector.tensor_tensor(w_lo[:, r, :], raw[:, r, :], w_hi[:, r, :].bitcast(f32), ALU.subtract).then_inc(lo_split, 1)

            def low(s, c):
                dve.wait_ge(h_hi_ready, KD * s + c + 1)
                nc.vector.scalar_tensor_tensor(out=h_lo[:, c, :], in0=x[:, c, :], scalar=pre_gain(s, c),
                                               in1=h_hi[:, c, :].bitcast(f32), op0=ALU.mult, op1=ALU.subtract).then_inc(h_ready, 1)

            def boundary(s):
                dve.wait_ge(rms_ready, 2 * s)
                dve.wait_ge(m_copied, KD * s)

                def scale(c):
                    wait(dve, x_ready, KD * (s - 1) + c - 1)
                    nc.vector.scalar_tensor_tensor(out=y[:, c % 2, :], in0=m[:, c, :], scalar=post_gain(s - 1, c),
                                                   in1=rms[:, 1, :], op0=ALU.mult, op1=ALU.mult).then_inc(y_scaled, 1)

                def add(c):
                    dve.wait_ge(y_scaled, KD * (s - 1) + c + 1)
                    nc.vector.tensor_tensor(x[:, c, :], x[:, c, :], y[:, c % 2, :], ALU.add).then_inc(x_ready, 1)
                scale(0)
                add(0)
                for c in range(KD):
                    if c + 1 < KD:
                        scale(c + 1)
                    if s < LAST:
                        low(s, c)
                    if c + 1 < KD:
                        add(c + 1)

            def ffn(s):
                u0 = first_unit[s]
                n0 = ffn_no[s] * KF

                def pair(u, n, b, first=False):
                    if first:
                        split(ahead(u, 4))
                        dve.wait_ge(rms_ready, 2 * s + 1)
                    dve.wait_ge(unit_used, count(u) + 1)
                    wait(dve, gate_silu, n0 + n)
                    nc.vector.tensor_tensor(gate[:], bank[b][:], rms[:, 0, :], ALU.mult).then_inc(gate_scaled, 1)
                    dve.wait_ge(unit_used, count(u) + 2)
                    wait(dve, act_mul, n0 + n)
                    nc.vector.tensor_tensor(up[:], bank[b + 1][:], rms[:, 0, :], ALU.mult).then_inc(up_scaled, 1)
                    if not first:
                        split(ahead(u, 4))
                    split(ahead(u, 5))
                    dve.wait_ge(act_hi_ready, n0 + n + 1)
                    nc.vector.tensor_tensor(act_lo[:, bass.ds(n, 1), :].rearrange("p a n -> p (a n)"), prod,
                                            act_hi[:, bass.ds(n, 1), :].rearrange("p a n -> p (a n)").bitcast(f32), ALU.subtract).then_inc(act_ready, 1)
                pair((u0, 0), 0, 0, True)
                pair((u0 + 2, 0), 1, 2)
                pair((u0 + 4, 0), 2, 5)
                pair((u0 + 6, 0), 3, 2)
                with dve.Fori(2, KF // 2) as i:
                    pair((u0, 4 * i), 2 * i, 0)
                    pair((u0 + 2, 4 * i), 2 * i + 1, 2)
                out_splits(s)

            def out_splits(s):
                kind = kinds[s]
                v0 = first_unit[s] + IN_UNITS[kind]
                n_out = N_UNITS[kind] - IN_UNITS[kind]
                with dve.Fori(0, n_out if s < LAST - 1 else n_out - RING, RING) as i:
                    for q in range(RING):
                        split((v0 + RING + q, i))

            def by_chunk(t):
                return t[:].rearrange("p (n c) -> p n c", c=CH)

            def hgrn2(s):
                TT = nc.vector.tensor_tensor
                u0 = first_unit[s]
                dve.wait_ge(hg_loaded, N_HG)
                TT(bound_tmp[:, 1, :], bound_tmp[:, 0, :], bound_tmp[:, 0, :], ALU.subtract).then_inc(hg_const, 1)
                nc.vector.memset(scan_keep[:], 1.0).then_inc(hg_const, 1)
                nc.vector.memset(probs[:], 0.0).then_inc(hg_const, 1)
                dve.wait_ge(hg_const, 3)
                nc.vector.memset(by_chunk(scan_keep)[:, :, 0:1], 0.0).then_inc(hg_const, 1)
                dve.wait_ge(hg_const, 5)
                nc.vector.reciprocal(bound_tmp[:, 1, :], bound_tmp[:, 2, :]).then_inc(hg_const, 1)
                dve.wait_ge(hg_const, 6)
                TT(bound_tmp[:, 0, :], bound_tmp[:, 1, :], bound_tmp[:, 2, :], ALU.mult).then_inc(hg_const, 1)
                dve.wait_ge(hg_const, 7)
                TT(bound[:], bound_tmp[:, 0, :], bound_tmp[:, 0, :], ALU.subtract).then_inc(hg_const, 1)
                dve.wait_ge(hg_const, 8)
                nc.vector.tensor_scalar(bound_rest[:], bound[:], -1.0, 1.0, ALU.mult, ALU.add).then_inc(hg_const, 1)
                dve.wait_ge(ident_made, 4)
                nc.vector.memset(causal[:], 0.0).then_inc(hg_const, 1)
                dve.wait_ge(hg_const, 10)
                nc.vector.tensor_copy(causal[0:CH, 0:CH], upper[0:CH, 0:CH]).then_inc(hg_const, 1)
                nc.vector.tensor_copy(causal[CH:P, CH:P], upper[CH:P, CH:P]).then_inc(hg_const, 1)
                dve.wait_ge(hg_const, 12)
                dve.wait_ge(rms_ready, 2 * s + 1)
                r = rms[:, 0, :]

                def step(j, gemm, chain):
                    u = (u0, 4 * j) if not isinstance(j, int) else (u0 + 4 * j, 0)
                    tb = (0, 1, 0, 1) if chain else (0, 1, 2, 3)
                    TT = nc.vector.tensor_tensor
                    if chain:
                        dve.wait_ge(k_transposed, j)
                        wait(dve, ds_made, j - 1)
                        nc.vector.tensor_copy(k_tok[:].rearrange("p t v -> p (t v)"), bank[3][:]).then_inc(k_copied, 1)
                    if gemm:
                        dve.wait_ge(unit_used, count(u) + 1)
                        wait(dve, f_sig, j)
                        if chain:
                            wait(dve, o_made, j - 1)
                            dve.wait_ge(scores_made, j)
                        TT(f_in[:], bank[tb[0]][:], r, ALU.mult).then_inc(f_scaled, 1)
                    elif chain:
                        wait(dve, o_made, j - 1)
                        dve.wait_ge(scores_made, j)
                    if chain:
                        nc.vector.copy_predicated(probs[:], causal[:].bitcast(mybir.dt.uint32).unsqueeze(1).to_broadcast([P, NT, P]),
                                                  bank[5][:].rearrange("p (t c) -> p t c", c=P)).then_inc(probs_ready, 1)
                        dve.wait_ge(ds_made, j)
                        nc.vector.tensor_copy(state[:, 0, :], bank[6][:, 0:P]).then_inc(state_ready, 1)
                        for n in range(1, NCH - 1):
                            dve.wait_ge(state_ready, (NCH - 1) * (j - 1) + n)
                            nc.vector.scalar_tensor_tensor(out=state[:, n, :], in0=state[:, n - 1, :], scalar=e_all[:, n * CH + CH - 1:n * CH + CH],
                                                           in1=bank[6 + n % 2][:, n // 2 * P:(n // 2 + 1) * P],
                                                           op0=ALU.mult, op1=ALU.add).then_inc(state_ready, 1)
                    if gemm:
                        dve.wait_ge(f_sig, j + 1)
                        nc.vector.tensor_scalar(forget[:], sig[:], bound_rest[:, bass.ds(j, 1)], bound[:, bass.ds(j, 1)], ALU.mult, ALU.add).then_inc(forget_made, 1)
                        dve.wait_ge(forget_made, j + 1)
                        wait(dve, k_end_ready, j)
                        nc.vector.tensor_scalar(key[:], forget[:], -1.0, 1.0, ALU.mult, ALU.add).then_inc(key_made, 1)
                        split(ahead(u, 4))
                        dve.wait_ge(f_logged, j + 1)
                        wait(dve, all_ready, j)
                        nc.vector.tensor_tensor_scan(b[:], scan_keep[:], logf[:], 0.0, ALU.mult, ALU.add).then_inc(b_scanned, 1)
                        dve.wait_ge(b_scanned, j + 1)
                        wait(dve, neg_ready, j)
                        TT(by_chunk(b_mid), by_chunk(b), by_chunk(b)[:, :, CH // 2:CH // 2 + 1].to_broadcast([P, NCH, CH]), ALU.subtract).then_inc(b_centered, 1)
                        wait(dve, end_ready, j)
                        TT(by_chunk(b_end), by_chunk(b)[:, :, CH - 1:CH].to_broadcast([P, NCH, CH]), by_chunk(b), ALU.subtract).then_inc(b_ended, 1)
                        dve.wait_ge(unit_used, count(u) + 2)
                        wait(dve, v_transposed, j)
                        TT(v_fm[:], bank[tb[1]][:], r, ALU.mult).then_inc(i_scaled, 1)
                        split(ahead(u, 5))
                        dve.wait_ge(neg_ready, j + 1)
                        TT(k_cen[:], key[:], e_neg[:], ALU.mult).then_inc(k_cen_ready, 1)
                        split(ahead(u, 6))
                    if chain:
                        dve.wait_ge(o_root, j)
                        wait(dve, o_gated, j - 1)
                        nc.vector.scalar_tensor_tensor(out=osq[:], in0=bank[2][:], scalar=hg_gain[:], in1=o_rms[:], op0=ALU.mult, op1=ALU.mult).then_inc(o_normed, 1)
                        dve.wait_ge(o_normed, j)
                        wait(dve, o_ready, j - 1)
                        dve.wait_ge(g_silu, j)
                        TT(o_fm[:], osq[:], g_act[:], ALU.mult).then_inc(o_gated, 1)
                    if gemm:
                        dve.wait_ge(unit_used, count(u) + 3)
                        wait(dve, q_silu, j)
                        TT(q_in[:], bank[tb[2]][:], r, ALU.mult).then_inc(q_scaled, 1)
                    if chain:
                        dve.wait_ge(o_hi_ready, j)
                        TT(o_lo[:, bass.ds(j - 1, 1), :].rearrange("p a n -> p (a n)"), o_fm[:],
                           o_hi[:, bass.ds(j - 1, 1), :].rearrange("p a n -> p (a n)").bitcast(f32), ALU.subtract).then_inc(o_ready, 1)
                    if gemm:
                        dve.wait_ge(q_silu, j + 1)
                        TT(q_cen[:], q_act[:], e_pos[:], ALU.mult).then_inc(q_cen_ready, 1)
                        split(ahead(u, 7))
                        dve.wait_ge(unit_used, count(u) + 4)
                        wait(dve, g_silu, j)
                        TT(g_in[:], bank[tb[3]][:], r, ALU.mult).then_inc(g_scaled, 1)
                step(0, True, False)
                step(1, True, True)
                with dve.Fori(2, HEADS) as j:
                    step(j, True, True)
                step(HEADS, False, True)
                out_splits(s)

            def deltanet(s):
                TT = nc.vector.tensor_tensor
                r = rms[:, 0, :]

                def drain(j, i, b, d=None, pair=None):
                    u = gd_unit(s, i, d, pair)
                    dve.wait_ge(unit_used, count(u) + 1)
                    if i < 4:
                        wait(dve, conv_mac, 4 * (4 * j + i))
                        TT(pre[:, TAPS - 1:], bank[b][:], r, ALU.mult).then_inc(drained, 1)
                    else:
                        dve.wait_ge(qkv_silu, 4 * j + i - 1)
                        TT((gate, up)[i % 2][:], bank[b][:], r, ALU.mult).then_inc(drained, 1)

                def mac(j, i, tap):
                    dst = (gate, up)[i % 2][:]
                    w = conv_w[:, bass.ds(j, 1), i, tap:tap + 1].rearrange("p a b -> p (a b)")
                    if tap == 0:
                        dve.wait_ge(drained, 2 + i + (6 * j if not isinstance(j, int) else 6 * j))
                        if i < 2:
                            wait(dve, z_silu, 2 * (j - 1) + i + 1)
                        else:
                            dve.wait_ge(qkv_silu, 4 * j + i - 1)
                        nc.vector.tensor_scalar(dst, pre[:, 0:TOK], w, None, ALU.mult).then_inc(conv_mac, 1)
                    else:
                        dve.wait_ge(conv_mac, 4 * (4 * j + i) + tap)
                        nc.vector.scalar_tensor_tensor(out=dst, in0=pre[:, tap:tap + TOK], scalar=w, in1=dst,
                                                       op0=ALU.mult, op1=ALU.add).then_inc(conv_mac, 1)

                def lo(i, d, pair):
                    split(ahead(gd_unit(s, i, d, pair), 4))

                def betas():
                    nc.vector.memset(inv[:], 0.0).then_inc(ab_dve, 1)
                    nc.vector.memset(keep_rows, 1.0)
                    dve.wait_ge(rms_ready, 2 * s + 1)
                    dve.wait_ge(ab_dve, 1)
                    TT(ab_in, bank[0][0:AB, :], rms[0:AB, 0, :], ALU.mult).then_inc(drained, 1)
                    dve.wait_ge(drained, 1)
                    nc.vector.memset(keep_rows.rearrange("p (t c) -> p t c", c=P)[:, :, 0:1], 0.0)
                    nc.vector.tensor_scalar(ab_in[32:AB, :], ab_in[32:AB, :], gd_ab[32:AB, 0:1], None, ALU.add).then_inc(ab_dve, 1)
                    drain(0, 0, 1, 0, 0)
                    for tap in range(TAPS):
                        mac(0, 0, tap)
                    lo(0, 0, 0)
                    dve.wait_ge(ab_act, 5)
                    nc.vector.scalar_tensor_tensor(out=g_step[32:AB, :], in0=ab_in[32:AB, :], scalar=0.0, in1=ab_exp[32:AB, :],
                                                   op0=ALU.max, op1=ALU.add).then_inc(ab_dve, 1)
                    dve.wait_ge(ab_dve, 3)
                    nc.vector.tensor_scalar(g_step[32:AB, :], g_step[32:AB, :], ea[32:AB, :], -1.0, ALU.mult, ALU.mult).then_inc(ab_dve, 1)
                    dve.wait_ge(ab_dve, 4)
                    nc.vector.tensor_tensor_scan(g_row_tile[32:AB, :], keep_rows[32:AB, :], g_step[32:AB, :], 0.0, ALU.mult, ALU.add).then_inc(ab_dve, 1)
                    dve.wait_ge(ab_trans, 1)
                    src = bank[6][:, 0:NT * AB].rearrange("p (t h) -> p t h", h=AB)
                    nc.vector.tensor_copy(tab[:, 0, :, :], src[:, :, 32:AB]).then_inc(ab_dve, 1)
                    nc.vector.tensor_copy(tab[:, 2, :, :], src[:, :, 0:VH])
                    dve.wait_ge(ab_act, 6)
                    nc.vector.tensor_scalar(tab[:, 1, :, :], tab[:, 1, :, :], -1.0, None, ALU.mult).then_inc(ab_dve, 1)
                    dve.wait_ge(ab_dve, 7)
                    nc.vector.tensor_scalar(tab[:, 5, :, :], tab[:, 2, :, :], -1.0, None, ALU.mult).then_inc(ab_dve, 1)
                    dve.wait_ge(ab_act, 7)
                    dve.wait_ge(last_made, 1)
                    TT(tab[:, 3, :, :], bank[7][:, 0:NT * VH].rearrange("p (t h) -> p t h", h=VH), tab[:, 0, :, :], ALU.subtract).then_inc(ab_dve, 1)
                    dve.wait_ge(ab_act, 8)
                    TT(tab[:, 3, :, :], tab[:, 3, :, :], tab[:, 2, :, :], ALU.mult).then_inc(ab_dve, 1)
                    dve.wait_ge(ab_dve, 10)

                def flat(x, e):
                    return x[:, e, :, :].rearrange("p t c -> p (t c)")

                def as_tiles(b):
                    return b[:].rearrange("p (t c) -> p t c", c=P)

                def wide(mask):
                    return mask.unsqueeze(1).to_broadcast([P, NT, P])

                def step(j, d, pair, gemm, chain):
                    g = j - 1
                    if chain:
                        wait(dve, vd_ready, 8 * g)
                        wait(dve, mem_ready, 6 * g)
                        wait(dve, vn_ready, 8 * g)
                        nc.vector.tensor_scalar(gtab[:], tab[:, :, :, bass.ds(2 * g, 2)], 1.0, None, ALU.mult).then_inc(gtab_ready, 1)
                        dve.wait_ge(gtab_ready, g + 1)
                        dve.wait_ge(g_loaded, 16 * (g + 1))
                        wait(dve, og_made, 2 * g)
                        for e in range(2):
                            for t in range(NT):
                                ins = nc.vector.tensor_scalar(attn[:, e, t, :], g_bc[:, e, t * P:(t + 1) * P], gtab[:, 0, t, e:e + 1], 0.0, ALU.subtract, ALU.min)
                            ins.then_inc(d_made, 1)
                        dve.wait_ge(qk_root, 2 * g + 1)
                        wait(dve, og_made, 2 * g)
                        nc.vector.scalar_tensor_tensor(out=qn, in0=q_a[:], scalar=float(P) ** -0.5, in1=y[:, 0, :], op0=ALU.mult, op1=ALU.mult).then_inc(qn_ready, 1)
                        dve.wait_ge(qk_root, 2 * g + 2)
                        TT(kn, k_a[:], y[:, 1, :], ALU.mult).then_inc(kn_ready, 1)
                        dve.wait_ge(kk_made, g + 1)
                        wait(dve, p_made, 12 * g)
                        for e in range(2):
                            dve.wait_ge(gam_ready, 2 * g + e + 1)
                            for t in range(NT):
                                ins = nc.vector.scalar_tensor_tensor(out=neg_at[:, e, t, :], in0=bank[7][:, t * P:(t + 1) * P], scalar=gtab[:, 5, t, e:e + 1],
                                                                     in1=attn[:, e, t, :], op0=ALU.mult, op1=ALU.mult)
                            ins.then_inc(at_ready, 1)
                            dve.wait_ge(at_ready, 2 * g + e + 1)
                            wait(dve, wr_made, 8 * g)
                            TT(inv_t[:, e, :, :], neg_at[:, e, :, :], wide(pair_mask[:]), ALU.mult).then_inc(xi_mul, 1)
                            dve.wait_ge(xi_mul, 2 * g + e + 1)
                            TT(inv_t[:, e, :, :], inv_t[:, e, :, :], wide(ident[:]), ALU.add).then_inc(x_init, 1)
                    if gemm:
                        drain(j, 0, 0, d, pair)
                    if chain:
                        dve.wait_ge(qk_made, g + 1)
                        for e in range(2):
                            TT(attn[:, e, :, :], attn[:, e, :, :], as_tiles(bank[2]), ALU.mult).then_inc(pt_ready, 1)
                    if gemm:
                        for tap in range(TAPS):
                            mac(j, 0, tap)
                    for l in range(1, LEVELS):
                        if chain:
                            for e in range(2):
                                if l < LEVELS - 1:
                                    dve.wait_ge(tt_made, 10 * g + 2 * (l - 1) + e + 1)
                                    nc.vector.memset(spare[:, e:e + 1], 0.0).then_inc(x_gate, 1)
                                    nc.vector.copy_predicated(inv[:, e, :, :], wide(low_mask[:, l, :]), as_tiles(bank[(7, 2)[e]])).then_inc(t_upd, 1)
                                else:
                                    dve.wait_ge(xx_made, 2 * g + e + 1)
                                    nc.vector.memset(spare[:, e:e + 1], 0.0).then_inc(x_gate, 1)
                                    nc.vector.copy_predicated(inv_t[:, e, :, :], wide(up_mask[:, l, :]), as_tiles(bank[3 + e])).then_inc(x_upd, 1)
                        if gemm and l == 1:
                            lo(0, d, pair)
                            drain(j, 1, 1, d, pair)
                            mac(j, 1, 0)
                        if gemm and l == 2:
                            for tap in range(1, TAPS):
                                mac(j, 1, tap)
                        if gemm and l == 3:
                            lo(1, d, pair)
                        if gemm and l == 5:
                            drain(j, 2, 0, d, pair)
                            for tap in range(TAPS - 1):
                                mac(j, 2, tap)
                        if gemm and l == 6:
                            mac(j, 2, TAPS - 1)
                    for t in range(NT):
                        if chain:
                            if t:
                                for e in range(2):
                                    dve.wait_ge(ks_made, 6 * g + 2 * (t - 1) + e + 1)
                                    dve.wait_ge(vt_ready, 2 * g + e + 1)
                                    nc.vector.scalar_tensor_tensor(out=resid_v[:, e, :], in0=bank[3 + e][:, 0:P], scalar=gtab[:, 1, t, e:e + 1],
                                                                   in1=vt[:, e, t, :], op0=ALU.mult, op1=ALU.add).then_inc(r_made, 1)
                            for e in range(2):
                                dve.wait_ge(wr_made, 8 * g + 2 * t + e + 1)
                                if t == 0:
                                    wait(dve, s_made, 6 * g)
                                nc.vector.tensor_scalar(v_dec[:, e, :], bank[5 + e][:, 0:P], gtab[:, 3, t, e:e + 1], None, ALU.mult).then_inc(vd_ready, 1)
                                nc.vector.tensor_scalar(v_new[:, e, :], bank[5 + e][:, 0:P], gtab[:, 2, t, e:e + 1], None, ALU.mult).then_inc(vn_ready, 1)
                        if gemm and t == 0:
                            lo(2, d, pair)
                        if gemm and t == 1:
                            drain(j, 3, 1, d, pair)
                        for tap in ((), (0,), (1,), (2, 3))[t] if gemm else ():
                            mac(j, 3, tap)
                        if chain and t < NT - 1:
                            for e in range(2):
                                dve.wait_ge(s_made, 6 * g + 2 * t + e + 1)
                                if t == 0:
                                    wait(dve, og_made, 2 * g)
                                    nc.vector.tensor_scalar(mem[:, e, 1, :], bank[3 + e][:, 0:P], 1.0, None, ALU.mult).then_inc(mem_ready, 1)
                                else:
                                    dve.wait_ge(mem_ready, 6 * g + 2 * t + e - 1)
                                    nc.vector.scalar_tensor_tensor(out=mem[:, e, (t + 1) % 2, :], in0=mem[:, e, t % 2, :], scalar=gtab[:, 4, t, e:e + 1],
                                                                   in1=bank[3 + e][:, 0:P], op0=ALU.mult, op1=ALU.add).then_inc(mem_ready, 1)
                    if gemm:
                        lo(3, d, pair)
                        drain(j, 4, 0, d, pair)
                    if chain:
                        for e in range(2):
                            dve.wait_ge(on_root, 2 * g + e + 1)
                            nc.vector.scalar_tensor_tensor(out=y[:, e, :], in0=bank[(7, 2)[e]][:], scalar=gd_gain[:], in1=y[:, e, :],
                                                           op0=ALU.mult, op1=ALU.mult).then_inc(og_normed, 1)
                            dve.wait_ge(og_normed, 2 * g + e + 1)
                            dve.wait_ge(z_silu, 2 * g + e + 1)
                            TT(gd_o[:, bass.ds(2 * g + e, 1), :].rearrange("p a n -> p (a n)"), y[:, e, :], z_a[:, e, :], ALU.mult).then_inc(og_ready, 1)
                    if gemm:
                        lo(4, d, pair)
                        drain(j, 5, 1, d, pair)
                        lo(5, d, pair)

                dve.wait_ge(ab_loaded, N_GD)
                nc.vector.memset(pre[:, 0:TAPS - 1], 0.0)
                split((first_unit[s] + RING, 0))
                betas()
                for i in range(1, 4):
                    drain(0, i, (1, 2, 3, 0)[i], 0, 0)
                    for tap in range(TAPS):
                        mac(0, i, tap)
                    if i < 3:
                        lo(i, 0, 0)
                lo(3, 0, 0)
                drain(0, 4, 1, 0, 0)
                lo(4, 0, 0)
                drain(0, 5, 0, 0, 0)
                lo(5, 0, 0)
                dve.wait_ge(masks_made, N_MASKS)
                step(1, 1, 0, True, True)
                with dve.Fori(0, GROUPS // 2 - 1) as k:
                    step(2 * k + 2, 2, k, True, True)
                    step(2 * k + 3, 3, k, True, True)
                step(GROUPS, 0, 0, False, True)
                dve.wait_ge(og_ready, VH)
                for k in range(VH):
                    dve.wait_ge(go_hi, k + 1)
                    dst, hi = (go_lo_a[:, k, :], h_hi[:, k, :]) if k < KD else (go_lo_b[:, k - KD, :], go_hi_b[:, k - KD, :])
                    TT(dst, gd_o[:, k, :], hi.bitcast(f32), ALU.subtract).then_inc(go_ready, 1)
                out_splits(s)

            nc.vector.memset(ones[:], 1.0).then_inc(const_made, 1)
            nc.vector.memset(eps[:], 1e-6).then_inc(const_made, 1)
            dve.wait_ge(const_loaded, N_CONST)
            nc.vector.tensor_scalar(half_gains[:], gains[:], 0.5, None, ALU.mult).then_inc(const_made, 1)
            dve.wait_ge(const_made, 3)
            for c in range(KD):
                cols = slice(c * P, (c + 1) * P)
                dve.wait_ge(hi_split, c + 1)
                nc.vector.tensor_tensor(w_lo[:, :, cols], raw[:, :, cols], w_hi[:, :, cols].bitcast(f32), ALU.subtract).then_inc(lo_split, 1)
                low(0, c)
            for s, kind in enumerate(kinds):
                {"ffn": ffn, "hg": hgrn2, "gd": deltanet}[kind](s)
                boundary(s + 1)

        @block.gpsimd
        def _(pool):
            def total(q, c, par, first=False):
                pool.wait_ge(sq_done, KD * q + c + 1)
                if first:
                    wait(pool, sum_ready, q)
                    nc.gpsimd.tensor_copy(acc[:], sq[:, par, :]).then_inc(acc_done, 1)
                else:
                    pool.wait_ge(acc_done, POOLED * q + c)
                    nc.gpsimd.tensor_tensor(acc[:], acc[:], sq[:, par, :], ALU.add).then_inc(acc_done, 1)

            def sum8(q):
                total(q, 0, 0, True)
                total(q, 1, 1)
                with pool.Fori(2, POOLED - 1, 2) as c:
                    total(q, c, 0)
                    total(q, c + 1, 1)
                total(q, POOLED - 1, (POOLED - 1) % 2)

            def ffn(s):
                n0 = ffn_no[s] * KF

                def product(n):
                    pool.wait_ge(gate_silu, n0 + n + 1)
                    pool.wait_ge(up_scaled, n0 + n + 1)
                    wait(pool, act_ready, n0 + n)
                    nc.gpsimd.tensor_tensor(prod, silu, up[:], ALU.mult).then_inc(act_mul, 1)
                product(0)
                with pool.Fori(1, KF) as n:
                    product(n)

            def hgrn2(s):
                def head(j):
                    pool.wait_ge(end_ready, j + 1)
                    pool.wait_ge(key_made, j + 1)
                    wait(pool, k_transposed, j)
                    nc.gpsimd.tensor_tensor(k_end[:], key[:], e_end[:], ALU.mult).then_inc(k_end_ready, 1)
                    pool.wait_ge(q_silu, j + 1)
                    wait(pool, o_made, j)
                    nc.gpsimd.tensor_tensor(q_int[:], q_act[:], e_all[:], ALU.mult).then_inc(q_int_ready, 1)
                head(0)
                with pool.Fori(1, HEADS) as j:
                    head(j)

            def deltanet(s):
                TTp = nc.gpsimd.tensor_tensor
                pool.wait_ge(sum_ready, 2 * s)
                nc.gpsimd.memset(low_mask[:], 1.0).then_inc(masks_made, 1)
                nc.gpsimd.memset(up_mask[:], 1.0).then_inc(masks_made, 1)
                nc.gpsimd.memset(pair_mask[:], 1.0).then_inc(masks_made, 1)
                made = 3
                cuts = []
                for l in range(LEVELS):
                    m = 1 << l
                    n = P // (2 * m)
                    lo_b, up_b = low_mask[:, l, :], up_mask[:, l, :]
                    for t, rows, cols in (((lo_b,), (m, 2 * m), (0, m)), ((up_b,) + ((pair_mask[:],) if l == 0 else ()), (0, m), (m, 2 * m))):
                        for dst in t:
                            cuts.append((dst, m, n, -rows[0], 1, [[-2 * m, n], [0, 2 * m]]))
                            cuts.append((dst, m, n, rows[1] - 1, -1, [[2 * m, n], [0, 2 * m]]))
                            if cols[0] == 0:
                                cuts.append((dst, m, n, m - 1, 0, [[0, n], [-1, 2 * m]]))
                            else:
                                cuts.append((dst, m, n, -m, 0, [[0, n], [1, 2 * m]]))
                for dst, m, n, base, cm, pattern in cuts:
                    pool.wait_ge(masks_made, made)
                    view = dst.rearrange("p (n r) -> p n r", r=2 * m)
                    nc.gpsimd.affine_select(out=view, in_=view, compare_op=ALU.is_ge, fill=0.0, base=base, pattern=pattern,
                                            channel_multiplier=cm).then_inc(masks_made, 1)
                    made += 1
                assert made == N_MASKS

                def group(g):
                    pool.wait_ge(eg_ready, g + 1)
                    pool.wait_ge(qn_ready, g + 1)
                    wait(pool, og_made, 2 * g)
                    for e in range(2):
                        TTp(q_g[:, e, :], qn, g_bc[:, e, :], ALU.mult).then_inc(qg_ready, 1)
                    for e in range(2):
                        pool.wait_ge(pt_ready, 2 * g + e + 1)
                        TTp(attn[:, e, :, :], attn[:, e, :, :], upper[:].unsqueeze(1).to_broadcast([P, NT, P]), ALU.mult).then_inc(pt_masked, 1)
                group(0)
                with pool.Fori(1, GROUPS) as g:
                    group(g)

            nc.gpsimd.memset(ident[:], 0.0).then_inc(ident_made, 1)
            nc.gpsimd.memset(upper[:], 1.0).then_inc(ident_made, 1)
            pool.wait_ge(ident_made, 2)
            nc.gpsimd.affine_select(out=ident[:], in_=ident[:], compare_op=ALU.not_equal, fill=1.0, base=0,
                                    pattern=[[-1, P]], channel_multiplier=1).then_inc(ident_made, 1)
            nc.gpsimd.affine_select(out=upper[:], in_=upper[:], compare_op=ALU.is_ge, fill=0.0, base=0,
                                    pattern=[[1, P]], channel_multiplier=-1).then_inc(ident_made, 1)
            for s, kind in enumerate(kinds):
                sum8(2 * s)
                {"ffn": ffn, "hg": hgrn2, "gd": deltanet}[kind](s)
                sum8(2 * s + 1)

        @block.tensor
        def _(pe):
            PASSES = ((0, 0), (0, 1), (1, 0))

            def sum_partitions(q):
                pe.wait_ge(acc_done, POOLED * (q + 1))
                wait(pe, rms_logged, q)
                nc.tensor.matmul(bank[4][:], ones[:], acc[:], start=True, stop=False)
                pe.wait_ge(sq_done, KD * (q + 1))
                nc.tensor.matmul(bank[4][:], ones[:], sq[:, POOLED % 2, :], start=False, stop=True).then_inc(sum_ready, 1)

            def blocks(dst, u, cols, moving, ks, first, last):
                r = u[0] % RING
                for n, k in enumerate(ks):
                    for wl, ml in PASSES:
                        w = (w_hi, w_lo)[wl][:, r, (cols + n) * P:(cols + n + 1) * P]
                        ins = nc.tensor.matmul(dst, w, moving[ml][:, k, :],
                                               start=first and n == 0 and (wl, ml) == (0, 0),
                                               stop=last and n == len(ks) - 1 and wl == 1)
                return ins

            def head_start(s):
                u0 = first_unit[s]
                if s:
                    pe.wait_ge(lo_split, u0 + RING + SKEW)
                for k in range(KD):
                    if s == 0:
                        pe.wait_ge(lo_split, k + 1)
                    pe.wait_ge(h_ready, KD * s + k + 1)
                    for q in range(RING):
                        ins = blocks(bank[q][:], (u0 + q, 0), k, (h_hi, h_lo), [k], k == 0, k == KD - 1)
                        if k == KD - 1:
                            ins.then_inc(unit_used, 1)
                            if q == 0:
                                sum_partitions(2 * s)

            def ffn(s):
                u0 = first_unit[s]
                n0 = ffn_no[s] * KF
                head_start(s)

                def four(i, banks):
                    for q in range(RING):
                        u = (u0 + q, 4 * i) if not isinstance(i, int) else (u0 + 4 * i + q, 0)
                        pe.wait_ge(lo_split, count(u) + 1 + SKEW)
                        if banks[q] < 5:
                            pe.wait_ge((gate_scaled, up_scaled)[q % 2], n0 + 2 * i + q // 2 - 1)
                        blocks(bank[banks[q]][:], u, 0, (h_hi, h_lo), range(KD), True, True).then_inc(unit_used, 1)
                four(1, (5, 6, 2, 3))
                with pe.Fori(2, 2 * KF // RING) as i:
                    four(i, (0, 1, 2, 3))

                def ready(k):
                    if k in (0, KF - 2, KF - 1):
                        pe.wait_ge(act_ready, n0 + max(k + 1, KF - 2))
                out_proj(s, (act_hi, act_lo), ready)

            def out_proj(s, moving, ready):
                cuts = CUTS[kinds[s]]
                n_u = len(cuts) - 1
                tiles = RING // n_u
                v0 = first_unit[s] + IN_UNITS[kinds[s]]

                def four(i, peeled=False):
                    for t in range(max(tiles, 2)):
                        c = tiles * i + t
                        if not peeled or t >= 2:
                            pe.wait_ge(m_copied, KD * s + c - 1)
                        for q in range(n_u):
                            k = t * n_u + q
                            u = (v0 + k, 4 * i) if not isinstance(i, int) else (v0 + k + 4 * i, 0)
                            pe.wait_ge(lo_split, count(u) + 1 + SKEW)
                            if peeled and t == 0:
                                for k in range(cuts[q], cuts[q + 1]):
                                    ready(k)
                                    ins = blocks(bank[t % 2][:], u, k - cuts[q], moving, [k], k == 0, k == cuts[-1] - 1)
                            else:
                                ins = blocks(bank[t % 2][:], u, 0, moving, range(cuts[q], cuts[q + 1]), q == 0, q == n_u - 1)
                            ins.then_inc(unit_used, 1)
                step = max(tiles, 2) // tiles
                four(0, True)
                with pe.Fori(step, KD // tiles, step) as i:
                    four(i)
                sum_partitions(2 * s + 1)

            def hgrn2(s):
                u0 = first_unit[s]
                MM = nc.tensor.matmul
                head_start(s)

                def step(j, gemm, chain):
                    first = isinstance(j, int)
                    free = (f_scaled if first else q_scaled, i_scaled if first else g_scaled, f_scaled, i_scaled)
                    at = [0]

                    def piece():
                        t, p = at[0] // 4, at[0] % 4
                        at[0] += 1
                        if not gemm or t == 4:
                            return
                        u = (u0 + t, 4 * j)
                        if p == 0:
                            pe.wait_ge(lo_split, count(u) + 1 + SKEW)
                            pe.wait_ge(free[t], j + (t >= 2))
                        ins = blocks(bank[t % 2][:], u, 2 * p, (h_hi, h_lo), [2 * p, 2 * p + 1], p == 0, p == 3)
                        if p == 3:
                            ins.then_inc(unit_used, 1)

                    piece()
                    if first:
                        for _ in range(4):
                            piece()
                    if chain:
                        pe.wait_ge(ident_made, 4)
                        pe.wait_ge(i_scaled, j)
                        pe.wait_ge(q_scaled, j)
                        wait(pe, o_normed, j - 1)
                        for t in range(NT):
                            ins = nc.tensor.transpose(bank[2][:, t * P:(t + 1) * P], v_fm[:, t * P:(t + 1) * P], ident[:])
                        ins.then_inc(v_transposed, 1)
                    piece()
                    if chain:
                        pe.wait_ge(k_cen_ready, j)
                        pe.wait_ge(q_cen_ready, j)
                        wait(pe, probs_ready, j - 1)
                        for t in range(NT):
                            ins = MM(bank[5][:, t * P:(t + 1) * P], k_cen[:, t * P:(t + 1) * P],
                                     q_cen[:, t * P:(t + 1) * P], start=True, stop=True)
                        ins.then_inc(scores_made, 1)
                        pe.wait_ge(k_end_ready, j)
                        pe.wait_ge(g_scaled, j)
                        wait(pe, o_logged, j - 1)
                        for t in range(NT):
                            ins = nc.tensor.transpose(bank[3][:, t * P:(t + 1) * P], k_end[:, t * P:(t + 1) * P], ident[:])
                        ins.then_inc(k_transposed, 1)
                    piece()
                    piece()
                    if chain:
                        pe.wait_ge(v_copied, j)
                        pe.wait_ge(k_copied, j)
                        wait(pe, state_ready, (NCH - 1) * (j - 1))
                        for n in range(NCH - 1):
                            r0 = n % 2 * CH
                            ins = MM(bank[6 + n % 2][:, n // 2 * P:(n // 2 + 1) * P], k_tok[r0:r0 + CH, n // 2, :],
                                     v_tok[r0:r0 + CH, n // 2, :], start=True, stop=True)
                        ins.then_inc(ds_made, 1)
                    for _ in range(4):
                        piece()
                    if chain:
                        pe.wait_ge(probs_ready, j)
                        pe.wait_ge(q_int_ready, j)
                        pe.wait_ge(state_ready, (NCH - 1) * j)
                        for t in range(NT):
                            MM(bank[2][:, t * P:(t + 1) * P], v_tok[:, t, :], probs[:, t, :], start=True, stop=False)
                            for n in (2 * t, 2 * t + 1):
                                if n:
                                    ins = MM(bank[2][:, n * CH:(n + 1) * CH], state[:, n - 1, :],
                                             q_int[:, n * CH:(n + 1) * CH], start=False, stop=n % 2 == 1)
                        ins.then_inc(o_made, 1)
                    for _ in range(3):
                        piece()
                    if chain:
                        pe.wait_ge(o_squared, j)
                        MM(bank[3][:], ones[:], osq[:], start=True, stop=True).then_inc(o_summed, 1)
                    piece()
                    for _ in range(4):
                        piece()
                step(1, True, True)
                with pe.Fori(2, HEADS) as j:
                    step(j, True, True)
                step(HEADS, False, True)

                def ready(k):
                    pe.wait_ge(o_ready, k + 1)
                out_proj(s, (o_hi, o_lo), ready)

            def deltanet(s):
                MM = nc.tensor.matmul
                head_start(s)
                u0 = first_unit[s]

                def tile(u, b, need):
                    pe.wait_ge(lo_split, count(u) + 1 + SKEW)
                    pe.wait_ge(drained, need)
                    blocks(bank[b][:], u, 0, (h_hi, h_lo), range(KD), True, True).then_inc(unit_used, 1)
                tile((u0 + 4, 0), 0, 1)
                tile((u0 + 5, 0), 1, 2)
                pe.wait_ge(ab_dve, 5)
                pe.wait_ge(ab_act, 1)
                for t in range(NT):
                    ins = nc.tensor.transpose(bank[6][:, t * AB:(t + 1) * AB], g_row_tile[:, t * P:(t + 1) * P], ident[0:AB, 0:AB])
                ins.then_inc(ab_trans, 1)
                pe.wait_ge(ab_dve, 6)
                MM(bank[7][:, 0:NT * VH], ident[:, P - 1:P].to_broadcast([P, P]), tab[:, 0, :, :].rearrange("p t h -> p (t h)"), start=True, stop=True).then_inc(last_made, 1)
                tile((u0 + 6, 0), 0, 5)

                def step(j, d, pair, gemm, chain):
                    g = j - 1
                    at = [0]

                    def piece(n=1):
                        if not gemm:
                            return
                        for _ in range(n):
                            i, p = at[0] // 6, at[0] % 6
                            at[0] += 1
                            u = gd_unit(s, i, d, pair)
                            if p == 0:
                                pe.wait_ge(lo_split, count(u) + 1 + SKEW)
                                pe.wait_ge(drained, 6 * j + i + (i == 0 and d == 1))
                            r = u[0] % RING
                            for x in range(4 * p, 4 * p + 4):
                                k, (wl, ml) = x // 3, PASSES[x % 3]
                                ins = MM(bank[i % 2][:], (w_hi, w_lo)[wl][:, r, k * P:(k + 1) * P], (h_hi, h_lo)[ml][:, k, :],
                                         start=x == 0, stop=x == 23)
                            if p == 5:
                                ins.then_inc(unit_used, 1)

                    def tiles(b, lhs, rhs, sem_):
                        for t in range(NT):
                            ins = MM(bank[b][:, t * P:(t + 1) * P], lhs(t), rhs(t), start=True, stop=True)
                        ins.then_inc(sem_, 1)

                    piece(4)
                    if chain:
                        for e in range(2):
                            pe.wait_ge(qk_squared, 2 * g + e + 1)
                            wait(pe, og_normed, 2 * g)
                            MM(bank[2 + e][:], ones[:], y[:, e, :], start=True, stop=True).then_inc(qk_summed, 1)
                    piece()
                    if chain:
                        for e in range(2):
                            pe.wait_ge(qkv_silu, 4 * (g + 1))
                            for t in range(NT):
                                ins = nc.tensor.transpose(bank[4 + e][:, t * P:(t + 1) * P], v_a[:, e, t * P:(t + 1) * P], ident[:])
                            ins.then_inc(v_trans, 1)
                    piece()
                    if chain:
                        pe.wait_ge(kn_ready, g + 1)
                        wait(pe, on_logged, 2 * g)
                        tiles(7, lambda t: kn[:, t * P:(t + 1) * P], lambda t: kn[:, t * P:(t + 1) * P], kk_made)
                        for t in range(NT):
                            ins = nc.tensor.transpose(bank[6][:, t * P:(t + 1) * P], kn[:, t * P:(t + 1) * P], ident[:])
                        ins.then_inc(k_trans, 1)
                        pe.wait_ge(qn_ready, g + 1)
                        tiles(2, lambda t: kn[:, t * P:(t + 1) * P], lambda t: qn[:, t * P:(t + 1) * P], qk_made)
                    piece(6)
                    if chain:
                        for e in range(2):
                            pe.wait_ge(x_init, 2 * g + e + 1)
                            pe.wait_ge(vt_ready, 2 * g + e + 1)
                            for t in range(NT):
                                ins = nc.tensor.transpose(bank[3 + e][:, t * P:(t + 1) * P], inv_t[:, e, t, :], ident[:])
                            ins.then_inc(x_trans, 1)
                    for l in range(1, LEVELS):
                        last = l == LEVELS - 1
                        if l == 1:
                            piece()
                        if chain:
                            for e in range(2):
                                if l > 1:
                                    pe.wait_ge(t_upd, 10 * g + 2 * (l - 2) + e + 1)
                                else:
                                    pe.wait_ge(t_ready, 2 * g + e + 1)
                                pe.wait_ge(kt_ready, g + 1)
                                pe.wait_ge(vt_ready, 2 * g + 2)
                                tiles(5 + e, lambda t: neg_at[:, e, t, :], lambda t: inv[:, e, t, :], p_made)
                                if l > 1:
                                    pe.wait_ge(t_ready, 2 * g + 2)
                                    if l > 2:
                                        pe.wait_ge(x_copied, 10 * g + 2 * (l - 3) + e + 1)
                                    for t in range(NT):
                                        ins = nc.tensor.transpose(bank[3 + e][:, t * P:(t + 1) * P], inv[:, e, t, :], ident[:])
                                    ins.then_inc(xt_made, 1)
                        piece()
                        if chain:
                            for e in range(2):
                                pe.wait_ge(p_ready, 12 * g + 2 * (l - 1) + e + 1)
                                if l > 1:
                                    pe.wait_ge(x_copied, 10 * g + 2 * (l - 2) + e + 1)
                                    pe.wait_ge(t_upd, 10 * g + 2 * (l - 1))
                                else:
                                    pe.wait_ge(pt_ready, 2 * g + 2)
                                if last:
                                    tiles(3 + e, lambda t: prod_at[:, e, t, :], lambda t: inv_t[:, e, t, :], xx_made)
                                else:
                                    tiles((7, 2)[e], lambda t: inv_t[:, e, t, :], lambda t: prod_at[:, e, t, :], tt_made)
                    for t in range(NT):
                        if t:
                            if chain:
                                for e in range(2):
                                    pe.wait_ge(mem_ready, 6 * g + 2 * (t - 1) + e + 1)
                                    MM(bank[3 + e][:, 0:P], kn[:, t * P:(t + 1) * P], mem[:, e, t % 2, :], start=True, stop=True).then_inc(ks_made, 1)
                        piece()
                        if chain:
                            for e in range(2):
                                if t:
                                    pe.wait_ge(r_made, 6 * g + 2 * (t - 1) + e + 1)
                                else:
                                    pe.wait_ge(x_upd, 2 * (g + 1))
                                rhs = resid_v[:, e, :] if t else vt[:, e, 0, :]
                                MM(bank[5 + e][:, 0:P], inv_t[:, e, t, :], rhs, start=True, stop=True).then_inc(wr_made, 1)
                            if t:
                                pe.wait_ge(qg_ready, 2 * (g + 1))
                                for e in range(2):
                                    MM(bank[(7, 2)[e]][:, t * P:(t + 1) * P], mem[:, e, t % 2, :], q_g[:, e, t * P:(t + 1) * P], start=True, stop=False)
                        piece()
                        if chain:
                            for e in range(2):
                                pe.wait_ge(vn_ready, 8 * g + 2 * t + e + 1)
                                pe.wait_ge(pt_masked, 2 * g + e + 1)
                                ins = MM(bank[(7, 2)[e]][:, t * P:(t + 1) * P], v_new[:, e, :], attn[:, e, t, :], start=t == 0, stop=True)
                                if t == NT - 1:
                                    ins.then_inc(og_made, 1)
                                else:
                                    pe.wait_ge(vd_ready, 8 * g + 2 * t + e + 1)
                                    MM(bank[3 + e][:, 0:P], kt[:, t * P:(t + 1) * P], v_dec[:, e, :], start=True, stop=True).then_inc(s_made, 1)
                        if t < NT - 1:
                            piece()
                    piece(2)
                    if chain:
                        for e in range(2):
                            pe.wait_ge(og_squared, 2 * g + e + 1)
                            MM(bank[5 + e][:], ones[:], y[:, e, :], start=True, stop=True).then_inc(on_summed, 1)
                    if gemm:
                        piece(36 - at[0])
                step(1, 1, 0, True, True)
                with pe.Fori(0, GROUPS // 2 - 1) as k:
                    step(2 * k + 2, 2, k, True, True)
                    step(2 * k + 3, 3, k, True, True)
                step(GROUPS, 0, 0, False, True)

                class Halves:
                    def __init__(self, a, b):
                        self.a, self.b = a, b

                    def __getitem__(self, at):
                        k = at[1]
                        return self.a[:, k, :] if k < KD else self.b[:, k - KD, :]

                def ready(k):
                    pe.wait_ge(go_ready, k + 1)
                out_proj(s, (Halves(h_hi, go_hi_b), Halves(go_lo_a, go_lo_b)), ready)

            for s, kind in enumerate(kinds):
                {"ffn": ffn, "hg": hgrn2, "gd": deltanet}[kind](s)


def pack_cols(np, w):
    k, n = w.shape
    return np.ascontiguousarray(w.reshape(k // P, P, n // P, P).transpose(2, 1, 0, 3)).reshape(n // P, P, k)



def kernel(**inputs):
    import numpy as np
    import concourse.bacc as bacc
    from concourse.bass_utils import run_bass_kernel_spmd

    a = {k: np.asarray(v) for k, v in inputs.items()}

    def in_ffn(w):
        return pack_cols(np, w).reshape(2, KF, P, UNIT).transpose(1, 0, 2, 3).reshape(2 * KF, P, UNIT)

    ffn_ins = (a["ffn1_w_in"][0], a["ffn2_w_in"][0], a["ffn1_w_in"][1], a["ffn2_w_in"][1])
    ffn_outs = (a["ffn1_w_out"][0], a["ffn2_w_out"][0], a["ffn1_w_out"][1], a["ffn2_w_out"][1])
    hg = pack_cols(np, a["hg_w_in"][0]).reshape(4, HEADS, P, UNIT)[[1, 2, 0, 3]].transpose(1, 0, 2, 3)
    gd = a["gd_w_in"][0]
    wide = 6 * GROUPS * P
    ab_w = np.zeros((D, P), gd.dtype)
    ab_w[:, 0:VH] = gd[:, wide:wide + VH]
    ab_w[:, AB - VH:AB] = gd[:, wide + VH:]
    order = [t for j in range(GROUPS) for t in (j, GROUPS + j, 2 * GROUPS + 2 * j, 2 * GROUPS + 2 * j + 1,
                                                4 * GROUPS + 2 * j, 4 * GROUPS + 2 * j + 1)]
    gd_tiles = pack_cols(np, np.ascontiguousarray(gd[:, :wide]))[order]
    conv_order = [t for t in order if t < 4 * GROUPS]
    ab_params = np.zeros((AB, 2), a["gd_dt_bias"].dtype)
    ab_params[AB - VH:, 0] = a["gd_dt_bias"][0]
    ab_params[AB - VH:, 1] = a["gd_a_log"][0]
    arrays = {
        "x": a["x"][0].T.reshape(KD, P, TOK).transpose(1, 0, 2),
        "gains": a["norm_gains"].reshape(12, KD, P).transpose(2, 0, 1).reshape(P, 12 * KD),
        "ffn_in": np.concatenate([in_ffn(w) for w in ffn_ins]),
        "ffn_out": np.concatenate([pack_cols(np, w) for w in ffn_outs]),
        "hg_in": hg.reshape(4 * HEADS, P, UNIT),
        "hg_out": pack_cols(np, a["hg_w_out"][0]),
        "hg_bounds": a["hg_lower_bounds"][0].reshape(HEADS, P).T,
        "hg_gain": a["hg_norm_gain"][0].reshape(P, 1),
        "gd_in": np.concatenate([pack_cols(np, ab_w), gd_tiles]),
        "gd_out": pack_cols(np, a["gd_w_out"][0]),
        "gd_conv": a["gd_conv_w"][0].reshape(TAPS, 4 * GROUPS, P)[:, conv_order].transpose(2, 1, 0).reshape(P, GROUPS, 4, TAPS),
        "gd_ab": ab_params,
        "gd_gain": a["gd_norm_gain"][0].reshape(P, 1),
    }
    arrays = {"in_" + k: np.ascontiguousarray(v) for k, v in arrays.items()}
    nc = bacc.Bacc("TRN2", target_bir_lowering=False, num_devices=1)
    A = {k[3:]: nc.dram_tensor(k, v.shape, mybir.dt.float32, kind="ExternalInput").ap() for k, v in arrays.items()}
    out = nc.dram_tensor("out", (P, KD, TOK), mybir.dt.float32, kind="ExternalOutput").ap()
    trunk(nc, A, out)
    got = run_bass_kernel_spmd(nc, [arrays], core_ids=[0]).results[0]["out"]
    return np.ascontiguousarray(got.transpose(1, 0, 2).reshape(D, TOK).T).reshape(1, TOK, D)
```
